# Optimizing a Trainium2 kernel written in Bass

```python
import math
import jax, jax.numpy as jnp
from jax import lax
import numpy as np

D_MODEL = 1024
BATCH = 1
SEQ = 1024
DEPTH = 1

DA_QK_DIM = 64
DA_V_DIM = 2 * DA_QK_DIM
DA_WIDTH = D_MODEL // 2
DA_HEADS = DA_WIDTH // DA_V_DIM
DA_QK_COLS = 2 * DA_HEADS * DA_QK_DIM
ROPE_DIM = DA_QK_DIM // 4
ROPE_THETA = 500000.0
Q_BLOCK = 128
ML_WIDTH = D_MODEL // 2
ML_HEADS = 4
ML_HEAD_DIM = ML_WIDTH // ML_HEADS
ML_CONV = 5
ML_CHUNK = 64
STAB_INIT = -1e30
N_BRANCH = 2
IN_SPLIT_SIZES = (DA_QK_COLS, DA_QK_COLS, DA_WIDTH,
                  ML_WIDTH, ML_WIDTH, ML_WIDTH, ML_WIDTH, 4 * ML_HEADS,
                  N_BRANCH * D_MODEL)
IN_COLS = sum(IN_SPLIT_SIZES)
N_KEYS = 128
N_EXPERTS = N_KEYS * N_KEYS
PEER_HEADS = 8
PEER_QDIM = 256
PEER_TOPK = 16
PEER_TOK_BLOCK = 128
DN_ALPHA = (2 * DEPTH) ** 0.25
DN_BETA = (8 * DEPTH) ** -0.25
LN_EPS = 1e-5

kernel_name = "hybrid_diffattn_mlstm_peer_encoder"

def layer_norm(x, g, b):
    xf = x.astype(jnp.float32)
    mu = xf.mean(-1, keepdims=True)
    var = jnp.square(xf - mu).mean(-1, keepdims=True)
    return ((xf - mu) * lax.rsqrt(var + LN_EPS) * g.astype(jnp.float32)
            + b.astype(jnp.float32)).astype(x.dtype)

def rms_norm(x, g):
    xf = x.astype(jnp.float32)
    y = xf * lax.rsqrt(jnp.mean(xf * xf, -1, keepdims=True) + LN_EPS)
    return (y * g.astype(jnp.float32)).astype(x.dtype)

def head_layer_norm(x, g):
    xf = x.astype(jnp.float32)
    mu = xf.mean(-1, keepdims=True)
    var = jnp.square(xf - mu).mean(-1, keepdims=True)
    y = (xf - mu) * lax.rsqrt(var + LN_EPS)
    return y.reshape(x.shape[:-2] + (-1,)) * g.astype(jnp.float32)

def partial_rope(t, cos, sin):
    half = ROPE_DIM // 2
    c = cos[None, :, None, None, :]
    s = sin[None, :, None, None, :]
    t1 = t[..., :half].astype(jnp.float32)
    t2 = t[..., half:ROPE_DIM].astype(jnp.float32)
    rot = jnp.concatenate([t1 * c - t2 * s, t2 * c + t1 * s], -1).astype(t.dtype)
    return jnp.concatenate([rot, t[..., ROPE_DIM:]], -1)

def diff_attention(q, k, v, lam_params, subln_g, lambda_init):
    B, S, H, _, Dq = q.shape
    lp = lam_params.astype(jnp.float32)
    lam = jnp.exp(jnp.sum(lp[0] * lp[1])) - jnp.exp(jnp.sum(lp[2] * lp[3])) + lambda_init
    nb = S // Q_BLOCK
    qb = (q * (Dq ** -0.5)).reshape(B, nb, Q_BLOCK, H, 2, Dq).transpose(1, 0, 3, 4, 2, 5)
    kh = k.transpose(0, 2, 3, 1, 4)
    vh = v.transpose(0, 2, 1, 3)

    def block(qblk):
        s = jnp.einsum('bhmqd,bhmkd->bhmqk', qblk, kh,
                       preferred_element_type=jnp.float32)
        p = jax.nn.softmax(s, axis=-1)
        a = p[:, :, 0] - lam * p[:, :, 1]
        return jnp.einsum('bhqk,bhkd->bhqd', a.astype(vh.dtype), vh)

    o = lax.map(block, qb)
    o = o.transpose(1, 0, 3, 2, 4).reshape(B, S, H, -1)
    o = rms_norm(o, subln_g) * (1.0 - lambda_init)
    return o.reshape(B, S, -1)

def mlstm_chunkwise(q, k, v, i_pre, log_f):
    B, H, S, D = q.shape
    nc = S // ML_CHUNK
    to_chunks = lambda t: jnp.moveaxis(t.reshape(B, H, nc, ML_CHUNK, *t.shape[3:]), 2, 0)
    qc, kc, vc = to_chunks(q), to_chunks(k), to_chunks(v)
    ic = to_chunks(i_pre)
    bc = jnp.cumsum(to_chunks(log_f), axis=-1)
    causal_in_chunk = jnp.tril(jnp.ones((ML_CHUNK, ML_CHUNK), bool))

    def step(carry, inp):
        C, n, m = carry
        qj, kj, vj, ij, bj = inp
        bL = bj[..., -1]
        dmat = jnp.where(causal_in_chunk, bj[..., :, None] - bj[..., None, :] + ij[..., None, :], -jnp.inf)
        inter = bj + m[..., None]
        m_row = jnp.maximum(inter, dmat.max(-1))
        w_inter = jnp.exp(inter - m_row)
        s = jnp.einsum('bhjd,bhld->bhjl', qj, kj) * jnp.exp(dmat - m_row[..., None])
        num = w_inter[..., None] * jnp.einsum('bhjd,bhde->bhje', qj, C) + jnp.einsum('bhjl,bhle->bhje', s, vj)
        den = w_inter * jnp.einsum('bhjd,bhd->bhj', qj, n) + s.sum(-1)
        h = num / jnp.maximum(jnp.abs(den), jnp.exp(-m_row))[..., None]
        g = bL[..., None] - bj + ij
        m_new = jnp.maximum(bL + m, g.max(-1))
        a = jnp.exp(bL + m - m_new)
        wk = jnp.exp(g - m_new[..., None])
        C = a[..., None, None] * C + jnp.einsum('bhl,bhld,bhle->bhde', wk, kj, vj)
        n = a[..., None] * n + jnp.einsum('bhl,bhld->bhd', wk, kj)
        return (C, n, m_new), h

    init = (jnp.zeros((B, H, D, D), jnp.float32), jnp.zeros((B, H, D), jnp.float32),
            jnp.full((B, H), STAB_INIT, jnp.float32))
    _, hs = lax.scan(step, init, (qc, kc, vc, ic, bc))
    return jnp.moveaxis(hs, 0, 2).reshape(B, H, S, D)

def depthwise_conv_centred(x, w, b):
    pad = (w.shape[0] - 1) // 2
    y = lax.conv_general_dilated(x, w[:, None, :].astype(x.dtype), window_strides=(1,),
                                 padding=[(pad, pad)], dimension_numbers=('NWC', 'WIO', 'NWC'),
                                 feature_group_count=x.shape[-1])
    return y + b

def mlstm_branch(ml_q, ml_k, ml_v, ml_o, ml_g, conv_w, conv_b, gate_b, norm_g):
    B, S, _ = ml_q.shape
    qk = jax.nn.silu(depthwise_conv_centred(jnp.concatenate([ml_q, ml_k], -1), conv_w, conv_b))
    q, k = jnp.split(qk.astype(jnp.float32), 2, axis=-1)
    heads = lambda t: t.reshape(B, S, ML_HEADS, ML_HEAD_DIM).transpose(0, 2, 1, 3)
    q, k, v = heads(q), heads(k) * (ML_HEAD_DIM ** -0.5), heads(ml_v.astype(jnp.float32))
    gates = (ml_g.astype(jnp.float32).reshape(B, S, 4, ML_HEADS)
             + gate_b.astype(jnp.float32)).transpose(2, 0, 3, 1)
    i_fw, f_fw, i_bw, f_bw = gates[0], gates[1], gates[2], gates[3]
    h_fw = mlstm_chunkwise(q, k, v, i_fw, jax.nn.log_sigmoid(f_fw))
    flip = lambda t: jnp.flip(t, axis=2)
    h_bw = flip(mlstm_chunkwise(flip(q), flip(k), flip(v), flip(i_bw), flip(jax.nn.log_sigmoid(f_bw))))
    h = (h_fw + h_bw).transpose(0, 2, 1, 3)
    h = head_layer_norm(h, norm_g) * jax.nn.sigmoid(ml_o.astype(jnp.float32))
    return h.astype(ml_q.dtype)

def peer(x, w_q, sub_keys, u_tab, v_tab):
    B, S, D = x.shape
    T = B * S
    xt = x.reshape(T, D)
    q = (xt @ w_q).reshape(T, PEER_HEADS, 2, PEER_QDIM // 2)
    s = jnp.einsum('thpd,pnd->thpn', q, sub_keys, preferred_element_type=jnp.float32)
    sc, idx = lax.top_k(s, PEER_TOPK)
    cand = (sc[:, :, 0, :, None] + sc[:, :, 1, None, :]).reshape(T, PEER_HEADS, -1)
    cand_idx = (idx[:, :, 0, :, None] * N_KEYS + idx[:, :, 1, None, :]).reshape(T, PEER_HEADS, -1)
    top_sc, top_pos = lax.top_k(cand, PEER_TOPK)
    experts = jnp.take_along_axis(cand_idx, top_pos, axis=-1)
    gates = jax.nn.softmax(top_sc, axis=-1)
    nb = T // PEER_TOK_BLOCK

    def block(args):
        xb, eb, gb = args
        act = jax.nn.gelu(jnp.einsum('ted,td->te', u_tab[eb], xb), approximate=False)
        return jnp.einsum('te,ted->td', gb * act, v_tab[eb])

    y = lax.map(block, (xt.reshape(nb, PEER_TOK_BLOCK, D),
                        experts.reshape(nb, PEER_TOK_BLOCK, -1),
                        gates.reshape(nb, PEER_TOK_BLOCK, -1).astype(x.dtype)))
    return y.reshape(B, S, D)

def setup_inputs(seed: int = 0) -> dict:
    key = jax.random.key(seed)
    ks = jax.random.split(key, 20)
    L, D = DEPTH, D_MODEL
    nrm = lambda k, shape, scale: jax.random.normal(k, shape, jnp.float32) * scale
    fbias = jnp.linspace(3.0, 6.0, ML_HEADS, dtype=jnp.float32)
    zb = jnp.zeros((ML_HEADS,), jnp.float32)
    gate_base = jnp.stack([zb, fbias, zb, fbias])[None]
    return {
        "x": nrm(ks[0], (BATCH, SEQ, D), 1.0),
        "w_in": nrm(ks[1], (L, D, IN_COLS), D ** -0.5),
        "da_lambda": nrm(ks[2], (L, 4, DA_QK_DIM), 0.1),
        "da_subln_g": 1.0 + nrm(ks[3], (L, DA_V_DIM), 0.02),
        "ml_conv_w": nrm(ks[4], (L, ML_CONV, 2 * ML_WIDTH), ML_CONV ** -0.5),
        "ml_conv_b": nrm(ks[5], (L, 2 * ML_WIDTH), 0.02),
        "ml_gate_b": gate_base + nrm(ks[6], (L, 4, ML_HEADS), 0.1),
        "ml_norm_g": 1.0 + nrm(ks[7], (L, ML_WIDTH), 0.02),
        "w_branch_attn": nrm(ks[8], (L, DA_WIDTH, D), DA_WIDTH ** -0.5),
        "w_branch_mlstm": nrm(ks[9], (L, ML_WIDTH, D), ML_WIDTH ** -0.5),
        "w_out": nrm(ks[10], (L, D, D), DN_BETA * D ** -0.5),
        "ln1_g": 1.0 + nrm(ks[11], (L, D), 0.02),
        "ln1_b": nrm(ks[12], (L, D), 0.02),
        "peer_w_q": nrm(ks[13], (L, D, PEER_HEADS * PEER_QDIM), D ** -0.5),
        "peer_sub_keys": nrm(ks[14], (L, 2, N_KEYS, PEER_QDIM // 2), (PEER_QDIM // 2) ** -0.5),
        "peer_u": nrm(ks[15], (L, N_EXPERTS, D), D ** -0.5),
        "peer_v": nrm(ks[16], (L, N_EXPERTS, D), DN_BETA),
        "ln2_g": 1.0 + nrm(ks[17], (L, D), 0.02),
        "ln2_b": nrm(ks[18], (L, D), 0.02),
    }

def reference(x, w_in, da_lambda, da_subln_g, ml_conv_w, ml_conv_b, ml_gate_b, ml_norm_g,
              w_branch_attn, w_branch_mlstm, w_out, ln1_g, ln1_b,
              peer_w_q, peer_sub_keys, peer_u, peer_v, ln2_g, ln2_b):
    B, S, D = x.shape
    split_at = [int(c) for c in np.cumsum(IN_SPLIT_SIZES)[:-1]]
    pos = jnp.arange(S, dtype=jnp.float32)
    inv_freq = ROPE_THETA ** (-jnp.arange(0, ROPE_DIM, 2, dtype=jnp.float32) / ROPE_DIM)
    ang = pos[:, None] * inv_freq[None, :]
    cos, sin = jnp.cos(ang), jnp.sin(ang)
    for l in range(DEPTH):
        lambda_init = 0.8 - 0.6 * math.exp(-0.3 * l)
        proj = x @ w_in[l]
        da_q, da_k, da_v, ml_q, ml_k, ml_v, ml_o, ml_g, br_g = jnp.split(proj, split_at, axis=-1)
        qa = partial_rope(da_q.reshape(B, S, DA_HEADS, 2, DA_QK_DIM), cos, sin)
        ka = partial_rope(da_k.reshape(B, S, DA_HEADS, 2, DA_QK_DIM), cos, sin)
        va = da_v.reshape(B, S, DA_HEADS, DA_V_DIM)
        y_attn = diff_attention(qa, ka, va, da_lambda[l], da_subln_g[l], lambda_init)
        y_mlstm = mlstm_branch(ml_q, ml_k, ml_v, ml_o, ml_g, ml_conv_w[l], ml_conv_b[l],
                               ml_gate_b[l], ml_norm_g[l])
        gates = jax.nn.sigmoid(br_g.reshape(B, S, N_BRANCH, D))
        merged = gates[:, :, 0] * (y_attn @ w_branch_attn[l]) + gates[:, :, 1] * (y_mlstm @ w_branch_mlstm[l])
        x = layer_norm(DN_ALPHA * x + (merged @ w_out[l]).astype(x.dtype), ln1_g[l], ln1_b[l])
        y_peer = peer(x, peer_w_q[l], peer_sub_keys[l], peer_u[l], peer_v[l])
        x = layer_norm(DN_ALPHA * x + y_peer.astype(x.dtype), ln2_g[l], ln2_b[l])
    return x


_drawn_inputs = setup_inputs


def setup_inputs(seed=0):
    import zlib

    import numpy as np

    out = dict(_drawn_inputs(seed))
    spreads = {}
    factors = {'da_subln_g': 3.19, 'ml_conv_b': 4.164, 'ml_norm_g': 4.091, 'ln2_g': 2.875, 'ln2_b': 2.903}
    for name, (base, spread) in spreads.items():
        noise = np.random.default_rng([zlib.crc32(name.encode()), seed]).standard_normal(out[name].shape)
        drawn = base * np.exp(spread * noise) if base else spread * noise
        out[name] = __import__('jax').numpy.asarray(drawn.astype(out[name].dtype))
    for name, factor in factors.items():
        out[name] = (out[name] * factor).astype(out[name].dtype)
    return out
```

```python
import math
import numpy as np
import concourse.bass as bass
from concourse import mybir
from contextlib import ExitStack

F32 = mybir.dt.float32
U32 = mybir.dt.uint32
ALU = mybir.AluOpType
ACT = mybir.ActivationFunctionType
AX = mybir.AxisListType

P = 128
SEQ = 1024
D_MODEL = 1024
TILES = SEQ // P
KT = D_MODEL // P
HALF = 512
N_KEYS = 128
TOPK = 16
PEER_HEADS = 8
LN_EPS = 1e-5
DN_ALPHA = 2 ** 0.25
NEG = -3.0e38


def at_least(engine, sem, value):
    if not (isinstance(value, int) and value <= 0):
        engine.wait_ge(sem, value)


class Chain:

    def __init__(self, engine, sem, passed=None):
        self.engine, self.sem, self.passed, self.start, self.n = engine, sem, passed, 0, 0

    def mark(self, instruction):
        instruction.then_inc(self.sem, 1)
        self.n += 1

    def wait(self):
        self.engine.wait_ge(self.sem, self.start + self.n)

    def step(self, instruction):
        self.mark(instruction)
        self.wait()

    def step_apart(self, instruction):
        self.step(instruction)
        self.engine.sem_inc(self.passed, 1)


U_RING = 8
V_RING = 8
DIAG_RING = 4
ROUTES = 4
DVE_FINISH_STEPS = 6


def peer_stage(nc, ctx, consts, x1t, x1_rows, w_q_dram, keys_t_dram, u_dram, v_dram, ln2_g_dram, ln2_b_dram, out_dram):
    def sb(name, shape, dt=F32):
        return ctx.enter_context(nc.sbuf_tensor(name, shape, dt))

    def ps(name, shape, dt=F32):
        return ctx.enter_context(nc.psum_tensor(name, shape, dt))

    def sem(name):
        return ctx.enter_context(nc.semaphore(name))

    ident, iota16 = consts["ident"], consts["iota16"]
    w_q = sb("w_q", [P, KT, 2 * PEER_HEADS * P])
    keys_t = sb("keys_t", [P, 2, N_KEYS])
    ln2_g = sb("ln2_g", [P, D_MODEL])
    ln2_b = sb("ln2_b", [P, D_MODEL])
    x_next = sb("x_next", [P, D_MODEL])
    x_tile = sb("x_tile", [P, D_MODEL])
    resid = sb("resid", [P, D_MODEL])
    u_rows = [sb(f"u_rows{r}", [P, D_MODEL]) for r in range(U_RING)]
    v_rows = [sb(f"v_rows{r}", [P, D_MODEL]) for r in range(V_RING)]
    q_t = sb("q_t", [P, 2, P])
    key_top = sb("key_top", [P, 2, TOPK])
    key_pos = sb("key_pos", [P, 2, TOPK], U32)
    key_pos_f = sb("key_pos_f", [P, 2, TOPK])
    rest = sb("rest", [P, 2, N_KEYS])
    cand = sb("cand", [P, TOPK, TOPK])
    cand_rest = sb("cand_rest", [P, TOPK * TOPK])
    top = sb("top", [P, ROUTES, TOPK])
    top_pos = sb("top_pos", [P, TOPK], U32)
    pos_half = sb("pos_half", [P, 2, TOPK], U32)
    pos_half_f = sb("pos_half_f", [P, 2, TOPK])
    one_hot = sb("one_hot", [P, 2, TOPK, TOPK])
    picked = sb("picked", [P, 2, TOPK])
    expert = [sb(f"expert{r}", [P, TOPK], U32) for r in range(ROUTES)]
    neg_max = sb("neg_max", [P, ROUTES])
    gate_e = sb("gate_e", [P, ROUTES, TOPK])
    gate_z = sb("gate_z", [P, ROUTES])
    gate_r = sb("gate_r", [P, ROUTES])
    dots = sb("dots", [P, ROUTES, TOPK])
    gelu = sb("gelu", [P, ROUTES, TOPK])
    weight = sb("weight", [P, ROUTES, TOPK])
    diag = sb("diag", [P, DIAG_RING, P])
    stats = sb("stats", [P, 2, 6])
    mean_var = sb("mean_var", [P, 2])
    rstd = sb("rstd", [P, 2])

    q_ps = ps("q_ps", [P, 2, P])
    score_ps = [ps(f"score_ps{r}", [P, 2, N_KEYS]) for r in range(2)]
    y_ps = [ps(f"y_ps{r}", [P, HALF]) for r in range(2)]

    weights_in = sem("d_weights_in")
    w_q_in = [sem(f"d_w_q_in{h}") for h in range(PEER_HEADS)]
    ln_in = sem("d_ln_in")
    x_in = sem("d_x_in")
    x_taken = sem("d_x_taken")
    q_ready = sem("d_q_ready")
    q_copied = sem("d_q_copied")
    scored = sem("d_scored")
    scores_read = sem("d_scores_read")
    routed = sem("d_routed")
    topped = sem("d_topped")
    gated = sem("d_gated")
    u_in = [sem(f"d_u_in{r}") for r in range(U_RING)]
    v_in = [sem(f"d_v_in{r}") for r in range(V_RING)]
    u_read = sem("d_u_read")
    gelu_done = sem("d_gelu_done")
    weighed = sem("d_weighed")
    diag_done = sem("d_diag_done")
    v_summed = sem("d_v_summed")
    y_read = sem("d_y_read")
    var_ready = sem("d_var_ready")
    std_ready = sem("d_std_ready")
    normed = sem("d_normed")
    stored = sem("d_stored")
    dve_chain = sem("d_dve_chain")
    dve_passed, pool_passed = sem("d_dve_passed"), sem("d_pool_passed")

    SLOTS = PEER_HEADS * TOPK
    def all_tiles(tile_program, engine):
        tile_program(0, True, False)
        with engine.Fori(1, TILES - 1) as tile:
            tile_program(tile, False, False)
        tile_program(TILES - 1, False, True)

    with nc.Block() as block:
        @block.sync
        def _(sp):
            sp.dma_start(x_next[:, :], x1_rows[0:P, :]).then_inc(x_in, 16)
            sp.dma_start(keys_t[:, :, :], keys_t_dram.rearrange("h d n -> d h n")).then_inc(weights_in, 16)
            w_q_view = w_q_dram.rearrange("(k p) n -> p k n", p=P)
            for h in range(PEER_HEADS):
                cols = slice(2 * h * P, 2 * (h + 1) * P)
                sp.dma_start(w_q[:, :, cols], w_q_view[:, :, cols]).then_inc(w_q_in[h], 16)
            sp.dma_start(ln2_g[:, :], ln2_g_dram.partition_broadcast(P)).then_inc(ln_in, 16)
            sp.dma_start(ln2_b[:, :], ln2_b_dram.partition_broadcast(P)).then_inc(ln_in, 16)

            def tile_program(tile, first, last):
                if not last:
                    sp.wait_ge(x_taken, tile + 1)
                    sp.dma_start(x_next[:, :], x1_rows[bass.ds((tile + 1) * P, P), :]).then_inc(x_in, 16)
                if not first:
                    sp.wait_ge(normed, tile)
                    sp.dma_start(out_dram[bass.ds((tile - 1) * P, P), :], resid[:, :]).then_inc(stored, 16)

            all_tiles(tile_program, sp)
            sp.wait_ge(normed, TILES)
            sp.dma_start(out_dram[(TILES - 1) * P:TILES * P, :], resid[:, :]).then_inc(stored, 16)
            sp.wait_ge(stored, 16 * TILES)

        @block.gpsimd
        def _(pool):
            def gather(rows, landed, table, route, slot):
                pool.sem_inc(pool_passed, 1)
                nc.gpsimd.indirect_dma_start(
                    rows[:, :], None, table, bass.IndirectOffsetOnAxis(ap=expert[route][:, slot:slot + 1], axis=0)
                ).then_inc(landed, 16)

            def gather_u(tile, h):
                pool.wait_ge(routed, tile * PEER_HEADS + h + 1)
                for s in range(TOPK):
                    at_least(pool, u_read, tile * SLOTS + h * TOPK + s - U_RING + 1)
                    gather(u_rows[s % U_RING], u_in[s % U_RING], u_dram, h % ROUTES, s)

            def gather_v(tile, h):
                for s in range(TOPK):
                    at_least(pool, v_summed, tile * SLOTS + h * TOPK + s - V_RING + 1)
                    gather(v_rows[s % V_RING], v_in[s % V_RING], v_dram, h % ROUTES, s)

            def tile_program(tile, first, last):
                for h in range(PEER_HEADS):
                    if h + 1 < PEER_HEADS:
                        gather_u(tile, h + 1)
                    elif not last:
                        gather_u(tile + 1, 0)
                    gather_v(tile, h)

            gather_u(0, 0)
            all_tiles(tile_program, pool)

        @block.tensor
        def _(pe):
            def score(tile, h):
                n = tile * PEER_HEADS + h
                if isinstance(tile, int) and tile == 0:
                    pe.wait_ge(w_q_in[h], 16)
                at_least(pe, q_copied, n)
                for p in range(2):
                    for k in range(KT):
                        last = nc.tensor.matmul(q_ps[:, p, :], w_q[:, k, (2 * h + p) * P:(2 * h + p + 1) * P],
                                                x1t[:, k, bass.ds(tile * P, P)], start=(k == 0), stop=(k == KT - 1))
                last.then_inc(q_ready, 1)
                pe.wait_ge(q_copied, n + 1)
                at_least(pe, scores_read, n - 1)
                for p in range(2):
                    last = nc.tensor.matmul(score_ps[h % 2][:, p, :], q_t[:, p, :], keys_t[:, p, :],
                                            start=True, stop=True)
                last.then_inc(scored, 1)

            def sum_v(tile, h):
                for s in range(TOPK):
                    n = tile * SLOTS + h * TOPK + s
                    pe.wait_ge(diag_done, n + 1)
                    use = tile * (SLOTS // V_RING) + (h * TOPK + s) // V_RING + 1
                    pe.wait_ge(v_in[s % V_RING], use * 16)
                    for c in range(2):
                        last = nc.tensor.matmul(y_ps[c][:, :], diag[:, s % DIAG_RING, :],
                                                v_rows[s % V_RING][:, c * HALF:(c + 1) * HALF],
                                                start=(h == 0 and s == 0), stop=(h == PEER_HEADS - 1 and s == TOPK - 1))
                    last.then_inc(v_summed, 1)

            def tile_program(tile, first, last):
                for h in range(PEER_HEADS):
                    if h + 2 < PEER_HEADS:
                        score(tile, h + 2)
                    elif not last:
                        score(tile + 1, h + 2 - PEER_HEADS)
                    if h == 0:
                        at_least(pe, y_read, tile)
                    sum_v(tile, h)

            pe.wait_ge(weights_in, 16)
            score(0, 0)
            score(0, 1)
            all_tiles(tile_program, pe)

        @block.scalar
        def _(act):
            def copy_queries(tile, h):
                n = tile * PEER_HEADS + h
                act.wait_ge(q_ready, n + 1)
                at_least(act, scored, n)
                nc.scalar.activation(q_t[:, :, :], q_ps[:, :, :], ACT.Copy).then_inc(q_copied, 1)

            def exponentials(tile, h):
                r = h % ROUTES
                act.wait_ge(topped, tile * PEER_HEADS + h + 1)
                nc.scalar.activation(gate_e[:, r, :], top[:, r, :], ACT.Exp, bias=neg_max[:, r:r + 1],
                                     accum_out=gate_z[:, r:r + 1]).then_inc(gated, 1)

            def tile_program(tile, first, last):
                for h in range(PEER_HEADS):
                    r = h % ROUTES
                    n = tile * SLOTS + h * TOPK
                    act.wait_ge(u_read, n + TOPK)
                    nc.scalar.activation(gelu[:, r, :], dots[:, r, :], ACT.Gelu).then_inc(gelu_done, 1)
                    if h + 1 < PEER_HEADS:
                        exponentials(tile, h + 1)
                    elif not last:
                        exponentials(tile + 1, 0)
                    if h + 2 < PEER_HEADS:
                        copy_queries(tile, h + 2)
                    elif not last:
                        copy_queries(tile + 1, h + 2 - PEER_HEADS)
                    if h == 0 and not first:
                        root(tile - 1)
                    act.wait_ge(weighed, tile * PEER_HEADS + h + 1)
                    for s in range(TOPK):
                        at_least(act, v_summed, n + s - DIAG_RING + 1)
                        nc.scalar.activation(diag[:, s % DIAG_RING, :], ident[:, :], ACT.Copy,
                                             scale=weight[:, r, s:s + 1]).then_inc(diag_done, 1)

            def root(tile):
                act.wait_ge(var_ready, tile + 1)
                nc.scalar.activation(rstd[:, 1:2], rstd[:, 0:1], ACT.Sqrt).then_inc(std_ready, 1)

            copy_queries(0, 0)
            copy_queries(0, 1)
            exponentials(0, 0)
            all_tiles(tile_program, act)
            root(TILES - 1)

        @block.vector
        def _(dve):
            v = nc.vector
            def topk(chain, tile, h):
                n = tile * PEER_HEADS + h
                r = h % ROUTES
                dve.wait_ge(scored, n + 1)
                dve.sem_inc(dve_passed, 1)
                s_ps = score_ps[h % 2]
                for p in range(2):
                    last = v.max(key_top[:, p, 0:8], s_ps[:, p, :])
                chain.step_apart(last)
                for p in range(2):
                    v.max_index(key_pos[:, p, 0:8], key_top[:, p, 0:8], s_ps[:, p, :])
                for p in range(2):
                    last = v.match_replace(rest[:, p, :], key_top[:, p, 0:8], s_ps[:, p, :], NEG)
                chain.step_apart(last)
                for p in range(2):
                    last = v.max(key_top[:, p, 8:16], rest[:, p, :])
                last.then_inc(scores_read, 1)
                dve.wait_ge(scores_read, n + 1)
                dve.sem_inc(dve_passed, 1)
                for p in range(2):
                    last = v.max_index(key_pos[:, p, 8:16], key_top[:, p, 8:16], rest[:, p, :])
                sums = v.tensor_tensor(cand[:, :, :], key_top[:, 0, :].unsqueeze(2).to_broadcast([P, TOPK, TOPK]),
                                key_top[:, 1, :].unsqueeze(1).to_broadcast([P, TOPK, TOPK]), ALU.add)
                chain.step(sums)
                cand_f = cand[:, :, :].rearrange("p a b -> p (a b)")
                v.tensor_copy(key_pos_f[:, :, :], key_pos[:, :, :])
                at_least(dve, v_summed, (n - ROUTES + 1) * TOPK)
                dve.sem_inc(dve_passed, 1)
                chain.step_apart(v.max(top[:, r, 0:8], cand_f))
                v.max_index(top_pos[:, 0:8], top[:, r, 0:8], cand_f)
                chain.step_apart(v.match_replace(cand_rest[:, :], top[:, r, 0:8], cand_f, NEG))
                chain.step_apart(v.max(top[:, r, 8:16], cand_rest[:, :]))
                v.tensor_scalar(neg_max[:, r:r + 1], top[:, r, 0:1], -1.0, None, ALU.mult).then_inc(topped, 1)
                chain.step(v.max_index(top_pos[:, 8:16], top[:, r, 8:16], cand_rest[:, :]))
                v.tensor_scalar(pos_half[:, 0, :], top_pos[:, :], 4, None, ALU.logical_shift_right)
                chain.step(v.tensor_scalar(pos_half[:, 1, :], top_pos[:, :], 15, None, ALU.bitwise_and))
                chain.step(v.tensor_copy(pos_half_f[:, :, :], pos_half[:, :, :]))
                for p in range(2):
                    last = v.tensor_tensor(one_hot[:, p, :, :], pos_half_f[:, p, :].unsqueeze(2).to_broadcast([P, TOPK, TOPK]),
                                           iota16[:, :].unsqueeze(1).to_broadcast([P, TOPK, TOPK]), ALU.is_equal)
                chain.step(last)
                for p in range(2):
                    last = v.tensor_tensor(one_hot[:, p, :, :], one_hot[:, p, :, :],
                                           key_pos_f[:, p, :].unsqueeze(1).to_broadcast([P, TOPK, TOPK]), ALU.mult)
                chain.step(last)
                chain.step(v.tensor_reduce(picked[:, :, :], one_hot[:, :, :, :], AX.X, ALU.add))
                v.scalar_tensor_tensor(expert[r][:, :], picked[:, 0, :], float(N_KEYS), picked[:, 1, :],
                                       ALU.mult, ALU.add).then_inc(routed, 1)

            def dot(tile, h):
                r = h % ROUTES
                for s in range(TOPK):
                    use = tile * (SLOTS // U_RING) + (h * TOPK + s) // U_RING + 1
                    dve.wait_ge(u_in[s % U_RING], use * 16)
                    v.tensor_tensor_reduce(out=u_rows[s % U_RING][:, :], in0=u_rows[s % U_RING][:, :], in1=x_tile[:, :],
                                           scale=1.0, scalar=0.0, op0=ALU.mult, op1=ALU.add,
                                           accum_out=dots[:, r, s:s + 1]).then_inc(u_read, 1)

            def weigh(chain, tile, h):
                r = h % ROUTES
                n = tile * PEER_HEADS + h
                dve.wait_ge(gated, n + 1)
                chain.step(v.reciprocal(gate_r[:, r:r + 1], gate_z[:, r:r + 1]))
                dve.wait_ge(gelu_done, n + 1)
                v.scalar_tensor_tensor(weight[:, r, :], gelu[:, r, :], gate_r[:, r:r + 1], gate_e[:, r, :],
                                       ALU.mult, ALU.mult).then_inc(weighed, 1)

            def finish(chain, tile):
                dve.wait_ge(v_summed, (tile + 1) * SLOTS)
                for c in range(2):
                    last = v.tensor_tensor(resid[:, c * HALF:(c + 1) * HALF], resid[:, c * HALF:(c + 1) * HALF],
                                           y_ps[c][:, :], ALU.add)
                last.then_inc(y_read, 1)
                dve.wait_ge(y_read, tile + 1)
                for c in range(2):
                    last = v.bn_stats(stats[:, c, :], resid[:, c * HALF:(c + 1) * HALF])
                chain.step_apart(last)
                chain.step(v.bn_aggr(mean_var[:, :], stats[:, :, :].rearrange("p a b -> p (a b)")))
                v.tensor_scalar(rstd[:, 0:1], mean_var[:, 1:2], LN_EPS, None, ALU.add).then_inc(var_ready, 1)
                dve.wait_ge(std_ready, tile + 1)
                chain.step(v.reciprocal(rstd[:, 0:1], rstd[:, 1:2]))
                chain.step(v.tensor_scalar(resid[:, :], resid[:, :], mean_var[:, 0:1], rstd[:, 0:1], ALU.subtract, ALU.mult))
                dve.wait_ge(ln_in, 32)
                chain.step(v.tensor_tensor(resid[:, :], resid[:, :], ln2_g[:, :], ALU.mult))
                v.tensor_tensor(resid[:, :], resid[:, :], ln2_b[:, :], ALU.add).then_inc(normed, 1)


            def x_start(chain, tile, first):
                if not first:
                    at_least(dve, stored, (tile - 1) * 16)
                    chain.step(v.tensor_scalar(resid[:, :], x_tile[:, :], DN_ALPHA, None, ALU.mult))
                dve.wait_ge(x_in, (tile + 1) * 16)
                v.tensor_copy(x_tile[:, :], x_next[:, :]).then_inc(x_taken, 1)
                dve.wait_ge(x_taken, tile + 1)

            def tile_program(tile, first, last):
                chain.n = 0 if not first else chain.n
                if not first:
                    chain.start = first_steps + (tile - 1) * (first_steps - routed_steps + DVE_FINISH_STEPS)
                x_start(chain, tile, first)
                for h in range(PEER_HEADS):
                    dot(tile, h)
                    if h + 1 < PEER_HEADS:
                        topk(chain, tile, h + 1)
                    elif not last:
                        topk(chain, tile + 1, 0)
                    if h == 0 and not first:
                        finish(chain, tile - 1)
                    weigh(chain, tile, h)

            chain = Chain(dve, dve_chain, dve_passed)
            topk(chain, 0, 0)
            routed_steps = chain.n
            tile_program(0, True, False)
            first_steps = chain.n
            with dve.Fori(1, TILES - 1) as tile:
                tile_program(tile, False, False)
                assert chain.n == first_steps - routed_steps + DVE_FINISH_STEPS
            tile_program(TILES - 1, False, True)
            at_least(dve, stored, (TILES - 1) * 16)
            chain.step(v.tensor_scalar(resid[:, :], x_tile[:, :], DN_ALPHA, None, ALU.mult))
            finish(chain, TILES - 1)

DA_HEADS = 4
DA_DIM = 64
ROPE_HALF = 8
ROPE_THETA = 500000.0
BIG = 1.0e30
ML_HEADS = 4
ML_DIM = 128
CONV = 5
PAD = (CONV - 1) // 2
LAMBDA_INIT = 0.8 - 0.6 * math.exp(0.0)
WIDTH = 512
COL_DA_Q, COL_DA_K, COL_DA_V, COL_ML_Q, COL_ML_K, COL_ML_V, COL_ML_O = (WIDTH * i for i in range(7))
COL_GATES = 7 * WIDTH
COL_BRANCH = COL_GATES + 4 * ML_HEADS


class Stage:

    def __init__(self, nc, ctx, name):
        self.nc, self.ctx, self.name = nc, ctx, name

    def sb(self, name, shape, dt=F32):
        return self.ctx.enter_context(self.nc.sbuf_tensor(f"{self.name}_{name}", shape, dt))

    def ps(self, name, shape, dt=F32):
        return self.ctx.enter_context(self.nc.psum_tensor(f"{self.name}_{name}", shape, dt))

    def sem(self, name):
        return self.ctx.enter_context(self.nc.semaphore(f"{self.name}_{name}"))


def project_stage(nc, st, consts, x_t, ml, qkv, dram):
    ident = consts["ident"]
    w = [st.sb(f"w{r}", [P, KT, WIDTH]) for r in range(2)]
    w_gates = st.sb("w_gates", [P, KT, 16])
    gate_b = st.sb("gate_b", [P, 16])
    conv_w = st.sb("conv_w", [P, 2 * ML_HEADS, CONV])
    conv_b = st.sb("conv_b", [P, 2 * ML_HEADS])
    x_pad = [st.sb(f"x_pad{r}", [P, SEQ + 2 * PAD]) for r in range(2)]
    ROT = 3
    rot = [st.sb(f"rot{r}", [P, WIDTH]) for r in range(ROT)]
    turned = st.sb("turned", [P, 4, 8, ROPE_HALF])
    log_tmp = st.sb("log_tmp", [P, 3, TILES, 2, ML_HEADS])
    forget = ml["gates"][:, :, :].rearrange("p t (d k h) -> p t d k h", d=2, k=2)[:, :, :, 1, :]
    banks = [st.ps(f"bank{r}", [P, WIDTH]) for r in range(8)]

    x_in, small_in = st.sem("x_in"), st.sem("small_in")
    w_in = [st.sem(f"w_in{r}") for r in range(2)]
    pads_set = st.sem("pads_set")
    filled = st.sem("filled")
    act_copied = st.sem("act_copied")
    dve_copied = st.sem("dve_copied")
    padded = st.sem("padded")
    convolved = st.sem("convolved")
    rotated = st.sem("rotated")
    exp_done, ln_done, absf_done = st.sem("exp_done"), st.sem("ln_done"), st.sem("absf_done")
    silu_done = st.sem("silu_done")
    chain_sem = st.sem("chain")

    units = []
    for g in range(2):
        for c in range(4):
            units += [("conv", (g * 4 + c, half), "act") for half in range(2)]
    units.append(("gates", None, "dve"))
    turns = []
    for g in range(2):
        for t in range(TILES):
            units.append(("rope", (g, t), "act"))
            turns.append((g, t))
            if len(turns) > 2:
                units.append(("turn", turns.pop(0), "dve"))
    units += [("turn", turn, "dve") for turn in turns]
    units += [("v", t, "act") for t in range(TILES)]
    units += [("ml_v", t, "dve") for t in range(TILES)]
    units += [("ml_o", t, "act") for t in range(TILES)]
    blocks = [COL_ML_Q, COL_ML_K, COL_DA_Q, COL_DA_K, COL_DA_V, COL_ML_V, COL_ML_O]

    def block_of(kind, which):
        return {"conv": lambda: which[0] // 4, "rope": lambda: 2 + which[0], "v": lambda: 4,
                "ml_v": lambda: 5, "ml_o": lambda: 6}.get(kind, lambda: None)()

    last_of_block = {}
    for i, (kind, which, _) in enumerate(units):
        if block_of(kind, which) is not None:
            last_of_block[block_of(kind, which)] = i
    rope_order = [which for kind, which, _ in units if kind == "rope"]

    def emptied(i):
        return sum(e == units[i][2] for _, _, e in units[:i + 1])

    with nc.Block() as block:
        @block.sync
        def _(sp):
            w_view = dram["w_in"].rearrange("(k p) n -> p k n", p=P)
            for k in range(KT):
                sp.dma_start(x_t[:, k, :], dram["x_t"][k * P:(k + 1) * P, :]).then_inc(x_in, 16)
            sp.dma_start(w_gates[:, :, :], w_view[:, :, COL_GATES:COL_GATES + 16]).then_inc(small_in, 16)
            sp.dma_start(gate_b[:, :], dram["gate_b"].partition_broadcast(P)).then_inc(small_in, 16)
            sp.dma_start(conv_w[:, :, :], dram["conv_w"]).then_inc(small_in, 16)
            sp.dma_start(conv_b[:, :], dram["conv_b"]).then_inc(small_in, 16)
            for name in ("ident", "iota16", "cos", "sin", "mask", "pick"):
                sp.dma_start(consts[name][tuple(slice(None) for _ in consts[name].shape)], dram[name]).then_inc(small_in, 16)
            for i, col in enumerate(blocks):
                if i >= 2:
                    sp.wait_ge(filled, last_of_block[i - 2] + 1)
                sp.dma_start(w[i % 2][:, :, :], w_view[:, :, col:col + WIDTH]).then_inc(w_in[i % 2], 16)

        @block.gpsimd
        def _(pool):
            for r in range(2):
                nc.gpsimd.memset(x_pad[r][:, 0:PAD], 0.0)
                nc.gpsimd.memset(x_pad[r][:, SEQ + PAD:SEQ + 2 * PAD], 0.0).then_inc(pads_set, 1)
            nc.gpsimd.memset(ml["v"][:, :, :, ML_DIM:ML_DIM + 1], 1.0).then_inc(pads_set, 1)
            pool.wait_ge(pads_set, 3)

        SMALL = 16 * 10

        @block.tensor
        def _(pe):
            pe.wait_ge(x_in, 16 * KT)
            pe.wait_ge(small_in, SMALL)
            started = set()
            for i, (kind, which, engine) in enumerate(units):
                bank = banks[i % 8]
                if i >= 8:
                    pe.wait_ge(act_copied if units[i - 8][2] == "act" else dve_copied, emptied(i - 8))
                b = block_of(kind, which)
                if b is not None and b not in started:
                    started.add(b)
                    pe.wait_ge(w_in[b % 2], 16 * (b // 2 + 1))
                for k in range(KT):
                    flags = dict(start=(k == 0), stop=(k == KT - 1))
                    if kind == "conv":
                        c, half = which
                        last = nc.tensor.matmul(bank[:, :], w[b % 2][:, k, (c % 4) * P:(c % 4 + 1) * P],
                                                x_t[:, k, half * WIDTH:(half + 1) * WIDTH], **flags)
                    elif kind in ("rope", "v", "ml_v", "ml_o"):
                        t = which[1] if kind == "rope" else which
                        last = nc.tensor.matmul(bank[:, :], x_t[:, k, t * P:(t + 1) * P], w[b % 2][:, k, :], **flags)
                if kind == "gates":
                    for t in range(TILES):
                        for k in range(KT):
                            last = nc.tensor.matmul(bank[:, t * 16:(t + 1) * 16], x_t[:, k, t * P:(t + 1) * P],
                                                    w_gates[:, k, :], start=(k == 0), stop=(k == KT - 1))
                if kind == "turn":
                    n = rope_order.index(which)
                    pe.wait_ge(rotated, n + 1)
                    for c in range(4):
                        last = nc.tensor.transpose(bank[:, c * P:(c + 1) * P], rot[n % ROT][:, c * P:(c + 1) * P], ident[:, :])
                last.then_inc(filled, 1)

        def full(bank, parts):
            return bank[:, :].rearrange("p (a b) -> p a b", a=parts)

        @block.scalar
        def _(act):
            silus = 0

            def silu(c):
                act.wait_ge(convolved, c + 1)
                dst = (ml["q_t"] if c < 4 else ml["k_t"])[:, c % 4, :]
                nc.scalar.activation(dst, dst, ACT.Silu).then_inc(silu_done, 1)

            act.wait_ge(small_in, SMALL)
            for i, (kind, which, engine) in enumerate(units):
                if kind == "gates":
                    act.wait_ge(absf_done, 1)
                    nc.scalar.activation(log_tmp[:, 1, :, :, :], log_tmp[:, 0, :, :, :], ACT.Exp).then_inc(exp_done, 1)
                    act.wait_ge(exp_done, 1)
                    nc.scalar.activation(log_tmp[:, 2, :, :, :], log_tmp[:, 1, :, :, :], ACT.Ln, bias=1.0).then_inc(ln_done, 1)
                if engine != "act":
                    continue
                bank = banks[i % 8]
                act.wait_ge(filled, i + 1)
                if kind == "conv":
                    c, half = which
                    if c >= 2:
                        act.wait_ge(convolved, c - 1)
                    nc.scalar.activation(x_pad[c % 2][:, PAD + half * WIDTH:PAD + (half + 1) * WIDTH], bank[:, :],
                                         ACT.Copy).then_inc(act_copied, 1)
                elif kind == "rope":
                    n = rope_order.index(which)
                    if n >= ROT:
                        turned_unit = units.index(("turn", rope_order[n - ROT], "dve"))
                        act.wait_ge(filled, turned_unit + 1)
                    nc.scalar.activation(rot[n % ROT][:, :], bank[:, :], ACT.Copy).then_inc(act_copied, 1)
                elif kind == "v":
                    nc.scalar.activation(qkv["v"][:, which, :], bank[:, :], ACT.Copy).then_inc(act_copied, 1)
                elif kind == "ml_o":
                    nc.scalar.activation(ml["o"][:, which, :], bank[:, :], ACT.Sigmoid).then_inc(act_copied, 1)
                if kind == "v":
                    silu(silus)
                    silus += 1
            act.wait_ge(silu_done, 2 * ML_HEADS)

        @block.vector
        def _(dve):
            v = nc.vector
            chain = Chain(dve, chain_sem)
            acts = {i: emptied(i) for i, u in enumerate(units) if u[2] == "act"}
            dve.wait_ge(small_in, SMALL)
            dve.wait_ge(pads_set, 3)
            for i, (kind, which, engine) in enumerate(units):
                bank = banks[i % 8]
                if kind == "conv" and which[1] == 1:
                    c = which[0]
                    dve.wait_ge(act_copied, acts[i])
                    y = (ml["q_t"] if c < 4 else ml["k_t"])[:, c % 4, :]
                    row = x_pad[c % 2]
                    chain.step(v.tensor_scalar(y, row[:, 0:SEQ], conv_w[:, c, 0:1], conv_b[:, c:c + 1], ALU.mult, ALU.add))
                    for tap in range(1, CONV):
                        step = v.scalar_tensor_tensor(y, row[:, tap:tap + SEQ], conv_w[:, c, tap:tap + 1], y, ALU.mult, ALU.add)
                        if tap < CONV - 1:
                            chain.step(step)
                    step.then_inc(convolved, 1)
                if kind == "rope":
                    n = rope_order.index(which)
                    dve.wait_ge(act_copied, acts[i])
                    q = rot[n % ROT][:, :].rearrange("p (g d) -> p g d", d=DA_DIM)
                    low, high = q[:, :, 0:ROPE_HALF], q[:, :, ROPE_HALF:2 * ROPE_HALF]
                    cos = consts["cos"][:, which[1], :].unsqueeze(1).to_broadcast([P, 8, ROPE_HALF])
                    sin = consts["sin"][:, which[1], :].unsqueeze(1).to_broadcast([P, 8, ROPE_HALF])
                    for j, (a, b) in enumerate(((low, cos), (high, sin), (high, cos), (low, sin))):
                        last = v.tensor_tensor(turned[:, j, :, :], a, b, ALU.mult)
                    chain.step(last)
                    v.tensor_tensor(low, turned[:, 0, :, :], turned[:, 1, :, :], ALU.subtract)
                    v.tensor_tensor(high, turned[:, 2, :, :], turned[:, 3, :, :], ALU.add).then_inc(rotated, 1)
                    dve.wait_ge(rotated, n + 1)
                if engine != "dve":
                    continue
                dve.wait_ge(filled, i + 1)
                if kind == "gates":
                    v.tensor_tensor(ml["gates"][:, :, :], bank[:, 0:TILES * 16].rearrange("p (t g) -> p t g", g=16),
                                    gate_b[:, :].unsqueeze(1).to_broadcast([P, TILES, 16]), ALU.add).then_inc(dve_copied, 1)
                    dve.wait_ge(dve_copied, emptied(i))
                    chain.step(v.tensor_scalar(log_tmp[:, 0, :, :, :], forget, -1.0, None, ALU.mult))
                    v.tensor_tensor(log_tmp[:, 0, :, :, :], log_tmp[:, 0, :, :, :], forget, ALU.min).then_inc(absf_done, 1)
                elif kind == "turn":
                    g, t = which
                    v.tensor_copy((qkv["q_t"] if g == 0 else qkv["k_t"])[:, :, t * P:(t + 1) * P], full(bank, 4)).then_inc(dve_copied, 1)
                elif kind == "ml_v":
                    v.tensor_copy(ml["v"][:, which, :, 0:ML_DIM], full(bank, 4)).then_inc(dve_copied, 1)
            dve.wait_ge(ln_done, 1)
            chain.step(v.scalar_tensor_tensor(forget, forget, 0.0, log_tmp[:, 2, :, :, :], ALU.min, ALU.subtract))


def attention_stage(nc, st, consts, qkv, y_t, dram):
    ident = consts["ident"]
    SCORES, PROBS = 3, 4
    prob = [st.sb(f"prob{r}", [P, SEQ]) for r in range(PROBS)]
    diff_t = st.sb("diff_t", [P, TILES, P])
    o = st.sb("o", [P, TILES, DA_HEADS, P])
    square = st.sb("square", [P, P])
    sum_sq = st.sb("sum_sq", [P, TILES, DA_HEADS])
    rstd = st.sb("rstd", [P, 2, TILES, DA_HEADS])
    lam_in = st.sb("lam_in", [P, 4, DA_DIM])
    lam_prod = st.sb("lam_prod", [P, 2, DA_DIM])
    lam = st.sb("lam", [P, 4])
    subln = st.sb("subln", [P, 2])
    top = st.sb("top", [P, PROBS])
    neg = st.sb("neg", [P, PROBS])
    z = st.sb("z", [P, PROBS])
    rz = st.sb("rz", [P, PROBS])
    score = [st.ps(f"score{r}", [P, SEQ]) for r in range(SCORES)]
    turn_ps = st.ps("turn_ps", [P, 4, P])
    o_ps = st.ps("o_ps", [P, WIDTH])

    small_in, lam_sum, lam_exp = st.sem("small_in"), st.sem("lam_sum"), st.sem("lam_exp")
    scored = st.sem("scored")
    maxed = st.sem("maxed")
    exped = st.sem("exped")
    combined = st.sem("combined")
    turned = st.sem("turned")
    turn_copied = st.sem("turn_copied")
    summed = st.sem("summed")
    o_copied = st.sem("o_copied")
    squared = st.sem("squared")
    meaned, rooted, scaled = st.sem("meaned"), st.sem("rooted"), st.sem("scaled")
    y_turned, y_copied = st.sem("y_turned"), st.sem("y_copied")
    chain_sem = st.sem("chain")
    PAIRS = DA_HEADS * TILES
    SCALE = DA_DIM ** -0.5

    with nc.Block() as block:
        @block.sync
        def _(sp):
            sp.dma_start(lam_in[:, :, :], dram["da_lambda"].partition_broadcast(P)).then_inc(small_in, 16)
            sp.dma_start(subln[:, 0:1], dram["da_subln_g"]).then_inc(small_in, 16)

        @block.tensor
        def _(pe):
            def scores(n, m):
                u = 2 * n + m
                h, t = n // TILES, n % TILES
                at_least(pe, exped, u - SCORES + 1)
                rows = slice(m * DA_DIM, (m + 1) * DA_DIM)
                for half in range(2):
                    last = nc.tensor.matmul(score[u % SCORES][:, half * WIDTH:(half + 1) * WIDTH],
                                            qkv["q_t"][rows, h, t * P:(t + 1) * P],
                                            qkv["k_t"][rows, h, half * WIDTH:(half + 1) * WIDTH], start=True, stop=True)
                last.then_inc(scored, 1)

            def turn(n, half):
                pe.wait_ge(combined, n + 1)
                at_least(pe, turn_copied, 2 * n + half)
                for i in range(4):
                    k = half * 4 + i
                    last = nc.tensor.transpose(turn_ps[:, i, :], prob[(2 * n) % PROBS][:, k * P:(k + 1) * P], ident[:, :])
                last.then_inc(turned, 1)

            scores(0, 0)
            scores(0, 1)
            scores(1, 0)
            for n in range(PAIRS):
                if n + 1 < PAIRS:
                    scores(n + 1, 1)
                turn(n, 0)
                if n + 2 < PAIRS:
                    scores(n + 2, 0)
                turn(n, 1)
                at_least(pe, o_copied, n)
                at_least(pe, squared, n)
                for k in range(TILES):
                    if k % 4 == 0:
                        pe.wait_ge(turn_copied, 2 * n + k // 4 + 1)
                    last = nc.tensor.matmul(o_ps[:, 0:P], diff_t[:, k, :], qkv["v"][:, k, (n // TILES) * P:(n // TILES + 1) * P],
                                            start=(k == 0), stop=(k == TILES - 1))
                last.then_inc(summed, 1)
            for t in range(TILES):
                pe.wait_ge(scaled, t + 1)
                at_least(pe, y_copied, t)
                for h in range(DA_HEADS):
                    last = nc.tensor.transpose(turn_ps[:, h, :], o[:, t, h, :], ident[:, :])
                last.then_inc(y_turned, 1)

        @block.scalar
        def _(act):
            def exponentials(n, m):
                u = 2 * n + m
                r = u % PROBS
                act.wait_ge(maxed, u + 1)
                if n >= 2:
                    act.wait_ge(turned, 2 * (n - 1))
                nc.scalar.activation(prob[r][:, :], score[u % SCORES][:, :], ACT.Exp, bias=neg[:, r:r + 1], scale=SCALE,
                                     accum_out=z[:, r:r + 1]).then_inc(exped, 1)

            def copy_turned(n, half):
                act.wait_ge(turned, 2 * n + half + 1)
                if half == 0:
                    at_least(act, summed, n)
                nc.scalar.activation(diff_t[:, 4 * half:4 * half + 4, :], turn_ps[:, :, :], ACT.Copy).then_inc(turn_copied, 1)

            act.wait_ge(lam_sum, 1)
            nc.scalar.activation(lam[:, 2:4], lam[:, 0:2], ACT.Exp).then_inc(lam_exp, 1)
            exponentials(0, 0)
            exponentials(0, 1)
            exponentials(1, 0)
            for n in range(PAIRS):
                copy_turned(n, 0)
                if n + 1 < PAIRS:
                    exponentials(n + 1, 1)
                copy_turned(n, 1)
                if n + 2 < PAIRS:
                    exponentials(n + 2, 0)
                h, t = n // TILES, n % TILES
                act.wait_ge(summed, n + 1)
                nc.scalar.activation(o[:, t, h, :], o_ps[:, 0:P], ACT.Copy).then_inc(o_copied, 1)
                nc.scalar.activation(square[:, :], o_ps[:, 0:P], ACT.Square,
                                     accum_out=sum_sq[:, t, h:h + 1]).then_inc(squared, 1)
            act.wait_ge(meaned, 1)
            nc.scalar.activation(rstd[:, 1, :, :], rstd[:, 0, :, :], ACT.Sqrt).then_inc(rooted, 1)
            for t in range(TILES):
                act.wait_ge(y_turned, t + 1)
                nc.scalar.activation(y_t[:, 0:DA_HEADS, t * P:(t + 1) * P], turn_ps[:, :, :], ACT.Copy,
                                     scale=subln[:, 1:2]).then_inc(y_copied, 1)

        @block.vector
        def _(dve):
            v = nc.vector
            chain = Chain(dve, chain_sem)

            def maximum(n, m):
                u = 2 * n + m
                r = u % PROBS
                dve.wait_ge(scored, u + 1)
                chain.step(v.reduce_max(top[:, r:r + 1], score[u % SCORES][:, :], AX.X))
                at_least(dve, exped, u - PROBS + 1)
                v.tensor_scalar(neg[:, r:r + 1], top[:, r:r + 1], -SCALE, None, ALU.mult).then_inc(maxed, 1)

            dve.wait_ge(small_in, 32)
            for i in range(2):
                last = v.tensor_tensor(lam_prod[:, i, :], lam_in[:, 2 * i, :], lam_in[:, 2 * i + 1, :], ALU.mult)
            chain.step(last)
            v.tensor_reduce(lam[:, 0:2], lam_prod[:, :, :], AX.X, ALU.add).then_inc(lam_sum, 1)
            dve.wait_ge(lam_exp, 1)
            chain.step(v.tensor_tensor(lam[:, 0:1], lam[:, 2:3], lam[:, 3:4], ALU.subtract))
            chain.step(v.tensor_scalar(lam[:, 1:2], lam[:, 0:1], -1.0, -LAMBDA_INIT, ALU.mult, ALU.add))
            v.tensor_scalar(subln[:, 1:2], subln[:, 0:1], 1.0 - LAMBDA_INIT, None, ALU.mult)
            maximum(0, 0)
            maximum(0, 1)
            maximum(1, 0)
            for n in range(PAIRS):
                a, b = (2 * n) % PROBS, (2 * n + 1) % PROBS
                dve.wait_ge(exped, 2 * n + 2)
                chain.step(v.reciprocal(rz[:, a:a + 2], z[:, a:a + 2]))
                v.tensor_scalar(prob[a][:, :], prob[a][:, :], rz[:, a:a + 1], None, ALU.mult)
                chain.step(v.tensor_scalar(rz[:, b:b + 1], rz[:, b:b + 1], lam[:, 1:2], None, ALU.mult))
                v.scalar_tensor_tensor(prob[a][:, :], prob[b][:, :], rz[:, b:b + 1], prob[a][:, :],
                                       ALU.mult, ALU.add).then_inc(combined, 1)
                if n + 1 < PAIRS:
                    maximum(n + 1, 1)
                if n + 2 < PAIRS:
                    maximum(n + 2, 0)
            dve.wait_ge(o_copied, PAIRS)
            dve.wait_ge(squared, PAIRS)
            v.tensor_scalar(rstd[:, 0, :, :], sum_sq[:, :, :], 1.0 / P, LN_EPS, ALU.mult, ALU.add).then_inc(meaned, 1)
            dve.wait_ge(rooted, 1)
            chain.step(v.reciprocal(rstd[:, 0, :, :], rstd[:, 1, :, :]))
            for t in range(TILES):
                v.tensor_tensor(o[:, t, :, :], o[:, t, :, :], rstd[:, 0, t, :].unsqueeze(2).to_broadcast([P, DA_HEADS, P]),
                                ALU.mult).then_inc(scaled, 1)


def shared(nc, ctx):
    st = Stage(nc, ctx, "all")
    consts = {"ident": st.sb("ident", [P, P]), "iota16": st.sb("iota16", [P, TOPK]),
              "cos": st.sb("cos", [P, TILES, ROPE_HALF]), "sin": st.sb("sin", [P, TILES, ROPE_HALF]),
              "mask": st.sb("mask", [P, 2, P]), "pick": st.sb("pick", [ML_HEADS, ML_HEADS, P])}
    mix_t = st.sb("mix_t", [P, KT, SEQ])
    return consts, mix_t


def shared_ml(nc, ctx):
    st = Stage(nc, ctx, "ml")
    return {"q_t": st.sb("q_t", [P, ML_HEADS, SEQ]), "k_t": st.sb("k_t", [P, ML_HEADS, SEQ]),
            "v": st.sb("v", [P, TILES, ML_HEADS, ML_DIM + 1]), "o": st.sb("o", [P, TILES, WIDTH]),
            "gates": st.sb("gates", [P, TILES, 16])}


def shared_qkv(nc, ctx):
    st = Stage(nc, ctx, "da")
    return {"q_t": st.sb("q_t", [P, DA_HEADS, SEQ]), "k_t": st.sb("k_t", [P, DA_HEADS, SEQ]),
            "v": st.sb("v", [P, TILES, WIDTH])}


def mlstm_stage(nc, st, consts, ml, y_t, dram):
    ident, mask, pick = consts["ident"], consts["mask"], consts["pick"]
    W_RING = 3
    run_max = [st.sb(f"run_max{d}", [ML_HEADS, SEQ]) for d in range(2)]
    u_cols = st.sb("u_cols", [P, 2, TILES, ML_HEADS])
    floor = st.sb("floor", [P, 2, TILES, ML_HEADS])
    norm_g = st.sb("norm_g", [P, ML_HEADS])

    with ExitStack() as rows_ctx:
        rows = Stage(nc, rows_ctx, "m_rows")
        i_row = [rows.sb(f"i{d}", [ML_HEADS, SEQ]) for d in range(2)]
        f_row = [rows.sb(f"f{d}", [ML_HEADS, SEQ]) for d in range(2)]
        b_row = [rows.sb(f"b{d}", [ML_HEADS, SEQ]) for d in range(2)]
        zeros = rows.sb("zeros", [ML_HEADS, SEQ])
        row_ps = [rows.ps(f"row{r}", [ML_HEADS, SEQ]) for r in range(3)]
        cols_ps = rows.ps("cols", [P, 2, 2, TILES, ML_HEADS])
        g_in, zeroed = rows.sem("g_in"), rows.sem("zeroed")
        turned, copied, ready, back, u_copied, chain_sem = (rows.sem(n) for n in ("turned", "copied", "ready", "back", "u_copied", "chain"))
        with nc.Block() as block:
            @block.sync
            def _(sp):
                sp.dma_start(norm_g[:, :], dram["ml_norm_g"]).then_inc(g_in, 16)
                sp.wait_ge(g_in, 16)

            @block.gpsimd
            def _(pool):
                nc.gpsimd.memset(zeros[:, :], 0.0).then_inc(zeroed, 1)

            @block.tensor
            def _(pe):
                for g in range(4):
                    if g == 3:
                        pe.wait_ge(copied, 1)
                    for t in range(TILES):
                        last = nc.tensor.transpose(row_ps[g % 3][:, t * P:(t + 1) * P],
                                                   ml["gates"][:, t, g * ML_HEADS:(g + 1) * ML_HEADS], ident[:, :])
                    last.then_inc(turned, 1)
                for d in range(2):
                    pe.wait_ge(ready, d + 1)
                    for t in range(TILES):
                        nc.tensor.transpose(cols_ps[:, 0, d, t, :], i_row[d][:, t * P:(t + 1) * P], ident[0:ML_HEADS, 0:ML_HEADS])
                        last = nc.tensor.transpose(cols_ps[:, 1, d, t, :], b_row[d][:, t * P:(t + 1) * P],
                                                   ident[0:ML_HEADS, 0:ML_HEADS])
                    last.then_inc(back, 1)

            @block.scalar
            def _(act):
                act.wait_ge(back, 2)
                act.wait_ge(u_copied, 1)
                nc.scalar.activation(floor[:, :, :, :], cols_ps[:, 1, :, :, :], ACT.Exp, scale=-1.0)

            @block.vector
            def _(dve):
                v = nc.vector
                chain = Chain(dve, chain_sem)
                for g in range(4):
                    dve.wait_ge(turned, g + 1)
                    dst = (i_row if g % 2 == 0 else f_row)[g // 2]
                    v.tensor_copy(dst[:, :], row_ps[g % 3][:, :]).then_inc(copied, 1)
                dve.wait_ge(copied, 4)
                dve.wait_ge(zeroed, 1)

                def along(row, d):
                    return row[:, :] if d == 0 else row[:, ::-1]

                for d in range(2):
                    chain.step(v.tensor_tensor_scan(along(b_row[d], d), along(f_row[d], d), zeros[:, :], 0.0, ALU.add, ALU.add))
                    chain.step(v.tensor_tensor(i_row[d][:, :], i_row[d][:, :], b_row[d][:, :], ALU.subtract))
                    chain.step(v.tensor_tensor_scan(along(run_max[d], d), along(i_row[d], d), along(i_row[d], d), NEG, ALU.max, ALU.max))
                    v.tensor_tensor(b_row[d][:, :], b_row[d][:, :], run_max[d][:, :], ALU.add).then_inc(ready, 1)
                dve.wait_ge(back, 2)
                v.tensor_copy(u_cols[:, :, :, :], cols_ps[:, 0, :, :, :]).then_inc(u_copied, 1)

    both = st.sb("both", [P, TILES, SEQ])
    diag_b = st.sb("diag_b", [P, TILES, P])
    max_b = [st.sb(f"max_b{d}", [P, SEQ]) for d in range(2)]
    max_diag = [st.sb(f"max_diag{d}", [P, TILES, P]) for d in range(2)]
    weight = [st.sb(f"weight{r}", [P, SEQ + P]) for r in range(W_RING)]
    h_sum = st.sb("h_sum", [P, TILES, ML_HEADS, ML_DIM])
    dens = [st.sb(f"den{r}", [P, 2]) for r in range(2)]
    stats = st.sb("stats", [P, TILES, ML_HEADS, 6])
    mean_var = st.sb("mean_var", [P, TILES, ML_HEADS, 2])
    rstd = st.sb("rstd", [P, 2, TILES, ML_HEADS])
    score = [st.ps(f"score{r}", [P, SEQ]) for r in range(2)]
    spread_ps = [st.ps(f"spread{r}", [P, WIDTH]) for r in range(2)]
    h_ps = [st.ps(f"h{r}", [P, 2, ML_DIM + 1]) for r in range(2)]
    names = "spread spread_copied masked weighed scored applied summed h_read std rooted gated turned y_copied chain normed".split()
    s = {n: st.sem(n) for n in names}
    K_SCALE = ML_DIM ** -0.5
    HT = ML_HEADS * TILES

    with nc.Block() as block:
        @block.tensor
        def _(pe):
            def spread(h):
                for i in range(4):
                    d, half = i // 2, i % 2
                    n = 4 * h + i
                    at_least(pe, s["spread_copied"], n - 1)
                    nc.tensor.matmul(spread_ps[n % 2][:, :], pick[:, h, :], run_max[d][:, half * WIDTH:(half + 1) * WIDTH],
                                     start=True, stop=True).then_inc(s["spread"], 1)

            def scores(h, i):
                n = h * TILES + i
                at_least(pe, s["applied"], n - 1)
                for half in range(2):
                    last = nc.tensor.matmul(score[n % 2][:, half * WIDTH:(half + 1) * WIDTH], ml["k_t"][:, h, i * P:(i + 1) * P],
                                            ml["q_t"][:, h, half * WIDTH:(half + 1) * WIDTH], start=True, stop=True)
                last.then_inc(s["scored"], 1)

            def sums(h, j):
                n = h * TILES + j
                at_least(pe, s["h_read"], n - 1)
                for l in range(j + 1):
                    nc.tensor.matmul(h_ps[n % 2][:, 0, :], both[:, l, j * P:(j + 1) * P], ml["v"][:, l, h, :],
                                     start=(l == 0), stop=(l == j))
                for l in range(j, TILES):
                    lhs = diag_b[:, l, :] if l == j else both[:, l, j * P:(j + 1) * P]
                    last = nc.tensor.matmul(h_ps[n % 2][:, 1, :], lhs, ml["v"][:, l, h, :], start=(l == j), stop=(l == TILES - 1))
                last.then_inc(s["summed"], 1)

            spread(0)
            for h in range(ML_HEADS):
                for i in range(TILES):
                    scores(h, i)
                if h + 1 < ML_HEADS:
                    spread(h + 1)
                pe.wait_ge(s["applied"], (h + 1) * TILES)
                for j in range(TILES):
                    sums(h, j)
            for t in range(TILES):
                pe.wait_ge(s["gated"], t + 1)
                at_least(pe, s["y_copied"], t - 1)
                for h in range(ML_HEADS):
                    last = nc.tensor.transpose(score[t % 2][:, h * P:(h + 1) * P], h_sum[:, t, h, :], ident[:, :])
                last.then_inc(s["turned"], 1)

        @block.scalar
        def _(act):
            for h in range(ML_HEADS):
                if h >= 1:
                    act.wait_ge(s["weighed"], TILES * h)
                    act.wait_ge(s["masked"], 2 * h)
                for i in range(4):
                    n = 4 * h + i
                    act.wait_ge(s["spread"], n + 1)
                    nc.scalar.activation(max_b[i // 2][:, (i % 2) * WIDTH:(i % 2 + 1) * WIDTH], spread_ps[n % 2][:, :],
                                         ACT.Copy).then_inc(s["spread_copied"], 1)
                act.wait_ge(s["spread_copied"], 4 * h + 4)
                act.wait_ge(s["masked"], 2 * h + 2)
                for i in range(TILES):
                    n = h * TILES + i
                    at_least(act, s["applied"], n - W_RING + 1)
                    w = weight[n % W_RING]
                    u = [u_cols[:, d, i, h:h + 1] for d in range(2)]
                    if i > 0:
                        nc.scalar.activation(w[:, 0:i * P], max_b[1][:, 0:i * P], ACT.Exp, bias=u[1], scale=-1.0)
                    if i + 1 < TILES:
                        nc.scalar.activation(w[:, (i + 1) * P:SEQ], max_b[0][:, (i + 1) * P:SEQ], ACT.Exp, bias=u[0], scale=-1.0)
                    nc.scalar.activation(w[:, i * P:(i + 1) * P], max_diag[0][:, i, :], ACT.Exp, bias=u[0], scale=-1.0)
                    nc.scalar.activation(w[:, SEQ:SEQ + P], max_diag[1][:, i, :], ACT.Exp, bias=u[1],
                                         scale=-1.0).then_inc(s["weighed"], 1)
            act.wait_ge(s["std"], 1)
            nc.scalar.activation(rstd[:, 1, :, :], rstd[:, 0, :, :], ACT.Sqrt).then_inc(s["rooted"], 1)
            for t in range(TILES):
                act.wait_ge(s["turned"], t + 1)
                for h in range(ML_HEADS):
                    last = nc.scalar.activation(y_t[:, ML_HEADS + h, t * P:(t + 1) * P], score[t % 2][:, h * P:(h + 1) * P],
                                                ACT.Copy, scale=norm_g[:, h:h + 1])
                last.then_inc(s["y_copied"], 1)

        @block.vector
        def _(dve):
            v = nc.vector
            chain = Chain(dve, s["chain"])
            for h in range(ML_HEADS):
                for d in range(2):
                    dve.wait_ge(s["spread_copied"], 4 * h + 2 * d + 2)
                    if h >= 1:
                        dve.wait_ge(s["weighed"], TILES * h)
                    v.tensor_tensor(max_diag[d][:, :, :], max_b[d][:, :].rearrange("p (t j) -> p t j", j=P),
                                    mask[:, d, :].unsqueeze(1).to_broadcast([P, TILES, P]), ALU.add).then_inc(s["masked"], 1)
                for i in range(TILES):
                    n = h * TILES + i
                    dve.wait_ge(s["scored"], n + 1)
                    dve.wait_ge(s["weighed"], n + 1)
                    at_least(dve, s["summed"], h * TILES)
                    v.scalar_tensor_tensor(diag_b[:, i, :], score[n % 2][:, i * P:(i + 1) * P], K_SCALE,
                                           weight[n % W_RING][:, SEQ:SEQ + P], ALU.mult, ALU.mult)
                    v.scalar_tensor_tensor(both[:, i, :], score[n % 2][:, :], K_SCALE, weight[n % W_RING][:, 0:SEQ],
                                           ALU.mult, ALU.mult).then_inc(s["applied"], 1)
                for j in range(TILES):
                    n = h * TILES + j
                    dve.wait_ge(s["summed"], n + 1)
                    at_least(dve, s["h_read"], n - 1)
                    bank, den = h_ps[n % 2], dens[n % 2]
                    chain.step(v.tensor_tensor(den[:, :], bank[:, :, ML_DIM], floor[:, :, j, h], ALU.max))
                    chain.step(v.scalar_tensor_tensor(den[:, :], bank[:, :, ML_DIM], -1.0, den[:, :], ALU.mult, ALU.max))
                    chain.step(v.reciprocal(den[:, :], den[:, :]))
                    chain.step(v.tensor_scalar(h_sum[:, j, h, :], bank[:, 0, 0:ML_DIM], den[:, 0:1], None, ALU.mult))
                    v.scalar_tensor_tensor(h_sum[:, j, h, :], bank[:, 1, 0:ML_DIM], den[:, 1:2], h_sum[:, j, h, :],
                                           ALU.mult, ALU.add).then_inc(s["h_read"], 1)
                dve.wait_ge(s["h_read"], (h + 1) * TILES)
            for j in range(TILES):
                for h in range(ML_HEADS):
                    last = v.bn_stats(stats[:, j, h, :], h_sum[:, j, h, :])
            chain.step(last)
            for j in range(TILES):
                for h in range(ML_HEADS):
                    last = v.bn_aggr(mean_var[:, j, h, :], stats[:, j, h, :])
            chain.step(last)
            v.tensor_scalar(rstd[:, 0, :, :], mean_var[:, :, :, 1], LN_EPS, None, ALU.add).then_inc(s["std"], 1)
            dve.wait_ge(s["rooted"], 1)
            chain.step(v.reciprocal(rstd[:, 0, :, :], rstd[:, 1, :, :]))
            for j in range(TILES):
                for h in range(ML_HEADS):
                    last = v.tensor_scalar(h_sum[:, j, h, :], h_sum[:, j, h, :], mean_var[:, j, h, 0:1], rstd[:, 0, j, h:h + 1],
                                           ALU.subtract, ALU.mult)
                chain.step(last)
                v.tensor_tensor(h_sum[:, j, :, :], h_sum[:, j, :, :], ml["o"][:, j, :].rearrange("p (h e) -> p h e", h=ML_HEADS),
                                ALU.mult).then_inc(s["gated"], 1)


def merge_stage(nc, st, consts, mix_t, dram, x1_rows):
    ident = consts["ident"]
    x_t = st.sb("x_t", [P, KT, SEQ])
    w_branch = [st.sb(f"w_branch{b}", [P, 4, D_MODEL]) for b in range(2)]
    merged = st.sb("merged", [P, KT, SEQ])
    w_gate = [st.sb(f"w_gate{r}", [P, KT, 2, P]) for r in range(2)]
    sig = st.sb("sig", [P, 2, WIDTH])
    prod = st.sb("prod", [P, 2, WIDTH])
    bank = [st.ps(f"bank{r}", [P, WIDTH]) for r in range(8)]
    x_in, w_in, ln_in, out_in, xr_in = (st.sem(n) for n in ("x_in", "w_in", "ln_in", "out_in", "xr_in"))
    g_in = [st.sem(f"g_in{r}") for r in range(2)]
    gate_full, branch_full, sig_done, mixed, merged_done, chain_sem = (
        st.sem(n) for n in ("gate_full", "branch_full", "sig_done", "mixed", "merged_done", "chain"))
    UNITS = 2 * KT

    with nc.Block() as block:
        @block.sync
        def _(sp):
            w_view = dram["w_in"].rearrange("(k p) n -> p k n", p=P)

            def gate_columns(c):
                if c >= 2:
                    sp.wait_ge(gate_full, 2 * (c - 1))
                for b in range(2):
                    col = COL_BRANCH + b * D_MODEL + c * P
                    sp.dma_start(w_gate[c % 2][:, :, b, :], w_view[:, :, col:col + P]).then_inc(g_in[c % 2], 16)

            gate_columns(0)
            for k in range(KT):
                sp.dma_start(x_t[:, k, :], dram["x_t"][k * P:(k + 1) * P, :]).then_inc(x_in, 16)
            for b, name in enumerate(("w_a", "w_m")):
                sp.dma_start(w_branch[b][:, :, :], dram[name].rearrange("(k p) n -> p k n", p=P)).then_inc(w_in, 16)
            for c in range(1, KT):
                gate_columns(c)

        @block.tensor
        def _(pe):
            pe.wait_ge(x_in, 16 * KT)
            for n in range(UNITS):
                c, half = n // 2, n % 2
                cols = slice(half * WIDTH, (half + 1) * WIDTH)
                at_least(pe, mixed, n - 1)
                pe.wait_ge(g_in[c % 2], 32 * (c // 2 + 1))
                for b in range(2):
                    for k in range(KT):
                        last = nc.tensor.matmul(bank[4 * (n % 2) + b][:, :], w_gate[c % 2][:, k, b, :], x_t[:, k, cols],
                                                start=(k == 0), stop=(k == KT - 1))
                last.then_inc(gate_full, 1)
                pe.wait_ge(w_in, 32)
                for b in range(2):
                    for k in range(4):
                        last = nc.tensor.matmul(bank[4 * (n % 2) + 2 + b][:, :], w_branch[b][:, k, c * P:(c + 1) * P],
                                                mix_t[:, 4 * b + k, cols], start=(k == 0), stop=(k == 3))
                last.then_inc(branch_full, 1)

        @block.scalar
        def _(act):
            for n in range(UNITS):
                act.wait_ge(gate_full, n + 1)
                at_least(act, mixed, n)
                for b in range(2):
                    last = nc.scalar.activation(sig[:, b, :], bank[4 * (n % 2) + b][:, :], ACT.Sigmoid)
                last.then_inc(sig_done, 1)

        @block.vector
        def _(dve):
            v = nc.vector
            for n in range(UNITS):
                c, half = n // 2, n % 2
                dve.wait_ge(branch_full, n + 1)
                dve.wait_ge(sig_done, n + 1)
                at_least(dve, merged_done, n)
                for b in range(2):
                    last = v.tensor_tensor(prod[:, b, :], sig[:, b, :], bank[4 * (n % 2) + 2 + b][:, :], ALU.mult)
                last.then_inc(mixed, 1)
                dve.wait_ge(mixed, n + 1)
                v.tensor_tensor(merged[:, c, half * WIDTH:(half + 1) * WIDTH], prod[:, 0, :], prod[:, 1, :],
                                ALU.add).then_inc(merged_done, 1)

    w_out = x_t
    ln_g, ln_b = w_branch[0][:, 0, :], w_branch[0][:, 1, :]
    x_row = [w_branch[1][:, r, :] for r in range(2)]
    r_row = [w_branch[1][:, 2 + r, :] for r in range(2)]
    stats = st.sb("stats", [P, 2, 6])
    mean_var = st.sb("mean_var", [P, 2])
    rstd = st.sb("rstd", [P, 2])
    full, read, var_done, rooted, normed, turned, turn_copied = (
        st.sem(n) for n in ("full", "read", "var_done", "rooted", "normed", "turned", "turn_copied"))
    xr = [st.sem(f"xr{r}") for r in range(2)]
    stored = [st.sem(f"stored{r}") for r in range(2)]
    with nc.Block() as block:
        @block.sync
        def _(sp):
            for k in range(KT):
                sp.dma_start(w_out[:, k, :], dram["w_out"][k * P:(k + 1) * P, :]).then_inc(out_in, 16)
            sp.dma_start(x_row[0], dram["x"][0:P, :]).then_inc(xr[0], 16)
            sp.dma_start(x_row[1], dram["x"][P:2 * P, :]).then_inc(xr[1], 16)
            sp.dma_start(ln_g, dram["ln1_g"].partition_broadcast(P)).then_inc(ln_in, 16)
            sp.dma_start(ln_b, dram["ln1_b"].partition_broadcast(P)).then_inc(ln_in, 16)
            for t in range(TILES):
                sp.wait_ge(normed, t + 1)
                sp.dma_start(x1_rows[t * P:(t + 1) * P, :], r_row[t % 2]).then_inc(stored[t % 2], 16)
                if t + 2 < TILES:
                    sp.dma_start(x_row[t % 2], dram["x"][(t + 2) * P:(t + 3) * P, :]).then_inc(xr[t % 2], 16)
            for r in range(2):
                sp.wait_ge(stored[r], 16 * TILES // 2)

        @block.tensor
        def _(pe):
            def turn(t):
                pe.wait_ge(normed, t + 1)
                for half in range(2):
                    n = 2 * t + half
                    at_least(pe, turn_copied, n - 1)
                    for i in range(4):
                        k = half * 4 + i
                        last = nc.tensor.transpose(bank[4 + half][:, i * P:(i + 1) * P], r_row[t % 2][:, k * P:(k + 1) * P], ident[:, :])
                    last.then_inc(turned, 1)

            pe.wait_ge(out_in, 16 * KT)
            for t in range(TILES):
                at_least(pe, read, t - 1)
                for half in range(2):
                    for k in range(KT):
                        last = nc.tensor.matmul(bank[2 * (t % 2) + half][:, :], merged[:, k, t * P:(t + 1) * P],
                                                w_out[:, k, half * WIDTH:(half + 1) * WIDTH], start=(k == 0), stop=(k == KT - 1))
                last.then_inc(full, 1)
                if t >= 1:
                    turn(t - 1)
            turn(TILES - 1)

        @block.scalar
        def _(act):
            for t in range(TILES):
                act.wait_ge(var_done, t + 1)
                nc.scalar.activation(rstd[:, 1:2], rstd[:, 0:1], ACT.Sqrt).then_inc(rooted, 1)
                for half in range(2):
                    act.wait_ge(turned, 2 * t + half + 1)
                    nc.scalar.activation(mix_t[:, 4 * half:4 * half + 4, t * P:(t + 1) * P],
                                         bank[4 + half][:, :].rearrange("p (k c) -> p k c", k=4), ACT.Copy).then_inc(turn_copied, 1)

        @block.vector
        def _(dve):
            v = nc.vector
            chain = Chain(dve, chain_sem)
            dve.wait_ge(ln_in, 32)
            for t in range(TILES):
                dve.wait_ge(full, t + 1)
                dve.wait_ge(xr[t % 2], 16 * (t // 2 + 1))
                at_least(dve, stored[t % 2], 16 * (t // 2))
                at_least(dve, turned, 2 * (t - 1))
                r = r_row[t % 2]
                for half in range(2):
                    cols = slice(half * WIDTH, (half + 1) * WIDTH)
                    last = v.scalar_tensor_tensor(r[:, cols], x_row[t % 2][:, cols], DN_ALPHA, bank[2 * (t % 2) + half][:, :],
                                                  ALU.mult, ALU.add)
                last.then_inc(read, 1)
                dve.wait_ge(read, t + 1)
                for half in range(2):
                    last = v.bn_stats(stats[:, half, :], r[:, half * WIDTH:(half + 1) * WIDTH])
                chain.step(last)
                chain.step(v.bn_aggr(mean_var[:, :], stats[:, :, :].rearrange("p a b -> p (a b)")))
                v.tensor_scalar(rstd[:, 0:1], mean_var[:, 1:2], LN_EPS, None, ALU.add).then_inc(var_done, 1)
                dve.wait_ge(rooted, t + 1)
                chain.step(v.reciprocal(rstd[:, 0:1], rstd[:, 1:2]))
                chain.step(v.tensor_scalar(r, r, mean_var[:, 0:1], rstd[:, 0:1], ALU.subtract, ALU.mult))
                chain.step(v.tensor_tensor(r, r, ln_g, ALU.mult))
                v.tensor_tensor(r, r, ln_b, ALU.add).then_inc(normed, 1)


def layer_program(nc, dram, u_table, v_table, x1_rows, out_rows):
    with ExitStack() as ctx:
        consts, mix_t = shared(nc, ctx)
        with ExitStack() as ml_ctx:
            ml = shared_ml(nc, ml_ctx)
            with ExitStack() as qkv_ctx:
                qkv = shared_qkv(nc, qkv_ctx)
                with ExitStack() as stage_ctx:
                    project_stage(nc, Stage(nc, stage_ctx, "proj"), consts, mix_t, ml, qkv, dram)
                with ExitStack() as stage_ctx:
                    attention_stage(nc, Stage(nc, stage_ctx, "attn"), consts, qkv, mix_t, dram)
            with ExitStack() as stage_ctx:
                mlstm_stage(nc, Stage(nc, stage_ctx, "mlstm"), consts, ml, mix_t, dram)
        with ExitStack() as stage_ctx:
            merge_stage(nc, Stage(nc, stage_ctx, "merge"), consts, mix_t, dram, x1_rows)
        with ExitStack() as stage_ctx:
            peer_stage(nc, stage_ctx, consts, mix_t, x1_rows, dram["w_q"], dram["keys_t"], u_table, v_table,
                       dram["ln2_g"], dram["ln2_b"], out_rows)


def shape_constants():
    position = np.arange(SEQ, dtype=np.float32)
    inv_freq = np.float32(ROPE_THETA) ** (-np.arange(0, 2 * ROPE_HALF, 2, dtype=np.float32) / np.float32(2 * ROPE_HALF))
    angle = (position[:, None] * inv_freq[None, :]).reshape(TILES, P, ROPE_HALF).transpose(1, 0, 2)
    step, row = np.arange(P)[:, None], np.arange(P)[None, :]
    mask = np.stack([np.where(row < step, BIG, 0.0), np.where(row > step, BIG, 0.0)], axis=1).astype(np.float32)
    pick = np.zeros((ML_HEADS, ML_HEADS, P), np.float32)
    for h in range(ML_HEADS):
        pick[h, h] = 1.0
    return {
        "ident": np.eye(P, dtype=np.float32),
        "iota16": np.ascontiguousarray(np.broadcast_to(np.arange(TOPK, dtype=np.float32), (P, TOPK))),
        "cos": np.ascontiguousarray(np.cos(angle)),
        "sin": np.ascontiguousarray(np.sin(angle)),
        "mask": mask,
        "pick": pick,
    }


def kernel(**inputs):
    import concourse.bacc as _bacc
    from concourse.bass_utils import run_bass_kernel_spmd as _run

    a = {name: np.asarray(value) for name, value in inputs.items()}
    x = a["x"][0]
    laid = {
        "x": x,
        "x_t": x.T,
        "w_in": a["w_in"][0],
        "gate_b": a["ml_gate_b"].reshape(4 * ML_HEADS),
        "conv_w": a["ml_conv_w"][0].T.reshape(2 * ML_HEADS, P, CONV).transpose(1, 0, 2),
        "conv_b": a["ml_conv_b"][0].reshape(2 * ML_HEADS, P).T,
        "da_lambda": a["da_lambda"][0],
        "da_subln_g": a["da_subln_g"][0].reshape(P, 1),
        "ml_norm_g": a["ml_norm_g"][0].reshape(ML_HEADS, P).T,
        "w_a": a["w_branch_attn"][0],
        "w_m": a["w_branch_mlstm"][0],
        "w_out": a["w_out"][0],
        "ln1_g": a["ln1_g"][0],
        "ln1_b": a["ln1_b"][0],
        "w_q": a["peer_w_q"][0],
        "keys_t": a["peer_sub_keys"][0].transpose(0, 2, 1),
        "u": a["peer_u"][0],
        "v": a["peer_v"][0],
        "ln2_g": a["ln2_g"][0],
        "ln2_b": a["ln2_b"][0],
        **shape_constants(),
    }
    nc = _bacc.Bacc("TRN2", target_bir_lowering=False, num_devices=1)
    arrays, dram = {}, {}
    for name, value in laid.items():
        arrays[f"in_{name}"] = np.ascontiguousarray(value)
        dram[name] = nc.dram_tensor(f"in_{name}", value.shape, F32, kind="ExternalInput").ap()
    x1_rows = nc.dram_tensor("x1_rows", (SEQ, D_MODEL), F32, kind="Internal").ap()
    out_rows = nc.dram_tensor("out_rows", (SEQ, D_MODEL), F32, kind="ExternalOutput").ap()
    layer_program(nc, dram, dram["u"], dram["v"], x1_rows, out_rows)
    result = _run(nc, [arrays], core_ids=[0])
    return result.results[0]["out_rows"].reshape(1, SEQ, D_MODEL)
```

```python
import math
import numpy as np
import concourse.bass as bass
from concourse import mybir
from contextlib import ExitStack

F32 = mybir.dt.float32
F32R = mybir.dt.float32r
U32 = mybir.dt.uint32
ALU = mybir.AluOpType
ACT = mybir.ActivationFunctionType
AX = mybir.AxisListType

P = 128
SEQ = 1024
D_MODEL = 1024
TILES = SEQ // P
KT = D_MODEL // P
HALF = 512
N_KEYS = 128
TOPK = 16
PEER_HEADS = 8
LN_EPS = 1e-5
DN_ALPHA = 2 ** 0.25
NEG = -3.0e38


def at_least(engine, sem, value):
    if not (isinstance(value, int) and value <= 0):
        engine.wait_ge(sem, value)


class Chain:

    def __init__(self, engine, sem, passed=None):
        self.engine, self.sem, self.passed, self.start, self.n = engine, sem, passed, 0, 0

    def mark(self, instruction):
        instruction.then_inc(self.sem, 1)
        self.n += 1

    def wait(self):
        self.engine.wait_ge(self.sem, self.start + self.n)

    def step(self, instruction):
        self.mark(instruction)
        self.wait()

    def step_apart(self, instruction):
        self.step(instruction)
        self.engine.sem_inc(self.passed, 1)


FIRST_TILES = 2
DENSE_TILES = 3
MID_TILES = TILES - FIRST_TILES - DENSE_TILES
N_DENSE = DENSE_TILES * P
DENSE_START = SEQ - N_DENSE
SLOTS = PEER_HEADS * TOPK


def route_stage(nc, st, consts, x1t, routes, dram, x1_rows, out_rows):
    U_RING, V_RING, DIAG_RING, SCORE_RING, GATES = 10, 8, 4, 4, 4
    ident, iota = consts["ident"], consts["iota"]
    w_q = st.sb("w_q", [P, KT, 2 * PEER_HEADS * P])
    keys_t = st.sb("keys_t", [P, 2, N_KEYS])
    ln2_g, ln2_b = st.sb("ln2_g", [P, D_MODEL]), st.sb("ln2_b", [P, D_MODEL])
    x_tile = st.sb("x_tile", [P, FIRST_TILES, D_MODEL])
    u_rows = [st.sb(f"u_rows{r}", [P, D_MODEL]) for r in range(U_RING)]
    v_rows = [st.sb(f"v_rows{r}", [P, D_MODEL]) for r in range(V_RING)]
    q_t = st.sb("q_t", [P, 2, P])
    key_top = st.sb("key_top", [P, 2, TOPK])
    key_pos = st.sb("key_pos", [P, 2, TOPK], U32)
    key_pos_f = st.sb("key_pos_f", [P, 2, TOPK])
    cand = st.sb("cand", [P, TOPK, TOPK])
    top_pos = st.sb("top_pos", [P, TOPK], U32)
    pos_half = st.sb("pos_half", [P, 2, TOPK], U32)
    pos_half_f = st.sb("pos_half_f", [P, 2, TOPK])
    one_hot = st.sb("one_hot", [P, 2, TOPK, TOPK])
    spare = one_hot[:, :, :, :].rearrange("p a b c -> p a (b c)")
    rest, cand_rest = spare[:, :, 0:N_KEYS], spare[:, 0, :]
    picked_here = st.sb("picked_here", [P, 2, TOPK])
    neg_max = st.sb("neg_max", [P, GATES])
    gate_e = st.sb("gate_e", [P, GATES, TOPK])
    gate_z = st.sb("gate_z", [P, GATES])
    gate_r = st.sb("gate_r", [P, GATES])
    dots = st.sb("dots", [P, GATES, TOPK])
    gelu = st.sb("gelu", [P, GATES, TOPK])
    weight = st.sb("weight", [P, GATES, TOPK])
    diag = st.sb("diag", [P, DIAG_RING, P])
    norm = LayerNormBuffers(st)
    sum_all = st.sb("sum_all", [P, TILES, PEER_HEADS])

    q_ps = st.ps("q_ps", [P, 2, P])
    score_ps = [st.ps(f"score_ps{r}", [P, 2, N_KEYS]) for r in range(SCORE_RING)]
    y_ps = [st.ps(f"y_ps{r}", [P, HALF]) for r in range(2)]

    keys_in, ln_in = st.sem("keys_in"), st.sem("ln_in")
    w_q_in = [st.sem(f"w_q_in{h}") for h in range(PEER_HEADS)]
    x_in = st.sem("x_in")
    q_ready = st.sem("q_ready")
    q_copied = st.sem("q_copied")
    scored = st.sem("scored")
    scores_read = st.sem("scores_read")
    routed = st.sem("routed")
    topped = st.sem("topped")
    gated = st.sem("gated")
    u_in = [st.sem(f"u_in{r}") for r in range(U_RING)]
    v_in = [st.sem(f"v_in{r}") for r in range(V_RING)]
    u_read = st.sem("u_read")
    gelu_done = st.sem("gelu_done")
    weighed = st.sem("weighed")
    diag_done = st.sem("diag_done")
    v_summed = st.sem("v_summed")
    y_read = st.sem("y_read")
    lessened, all_exp = st.sem("lessened"), st.sem("all_exp")
    normed, stored, chain_sem = st.sem("normed"), st.sem("stored"), st.sem("chain")

    own = [(t, h) for t in range(FIRST_TILES) for h in range(PEER_HEADS)]
    dense = range(TILES - DENSE_TILES, TILES)
    others = [(t, h) for t in (*dense, *range(FIRST_TILES, TILES - DENSE_TILES)) for h in range(PEER_HEADS)]
    each = len(others) // len(own)
    assert each * len(own) == len(others)
    batches = [own[:1]] + [own[n + 1:n + 2] + others[each * n:each * (n + 1)] for n in range(len(own))]
    order = [head for batch in batches for head in batch]
    place = {head: r for r, head in enumerate(order)}

    with nc.Block() as block:
        @block.sync
        def _(sp):
            w_q_view = dram["w_q"].rearrange("(k p) n -> p k n", p=P)
            sp.dma_start(keys_t[:, :, :], dram["keys_t"].rearrange("h d n -> d h n")).then_inc(keys_in, 16)
            for h in range(PEER_HEADS):
                cols = slice(2 * h * P, 2 * (h + 1) * P)
                sp.dma_start(w_q[:, :, cols], w_q_view[:, :, cols]).then_inc(w_q_in[h], 16)
                if h == 0:
                    sp.dma_start(x_tile[:, :, :], x1_rows[0:FIRST_TILES * P, :].rearrange("(t p) d -> p t d", p=P)).then_inc(x_in, 16)
            sp.dma_start(ln2_g[:, :], dram["ln2_g"].partition_broadcast(P)).then_inc(ln_in, 16)
            sp.dma_start(ln2_b[:, :], dram["ln2_b"].partition_broadcast(P)).then_inc(ln_in, 16)
            for t in range(FIRST_TILES):
                sp.wait_ge(normed, t + 1)
                sp.dma_start(out_rows[t * P:(t + 1) * P, :], x_tile[:, t, :]).then_inc(stored, 16)
            sp.wait_ge(stored, 16 * FIRST_TILES)

        @block.gpsimd
        def _(pool):
            def gather(n, s, rows, landed, table):
                t, h = own[n]
                at = h * TOPK + s
                nc.gpsimd.indirect_dma_start(
                    rows[:, :], None, table,
                    bass.IndirectOffsetOnAxis(ap=routes["expert"][:, t, at:at + 1], axis=0)).then_inc(landed, 16)

            def gather_u(n):
                pool.wait_ge(routed, place[own[n]] + 1)
                for s in range(TOPK):
                    at_least(pool, u_read, n * TOPK + s - U_RING + 1)
                    gather(n, s, u_rows[(n * TOPK + s) % U_RING], u_in[(n * TOPK + s) % U_RING], dram["u"])

            gather_u(0)
            for n in range(len(own)):
                if n + 1 < len(own):
                    gather_u(n + 1)
                for s in range(TOPK):
                    at_least(pool, v_summed, n * TOPK + s - V_RING + 1)
                    gather(n, s, v_rows[(n * TOPK + s) % V_RING], v_in[(n * TOPK + s) % V_RING], dram["v"])

        @block.tensor
        def _(pe):
            def score(head):
                t, h = head
                r = place[head]
                pe.wait_ge(w_q_in[h], 16)
                at_least(pe, q_copied, r)
                for p in range(2):
                    for k in range(KT):
                        last = nc.tensor.matmul(q_ps[:, p, :], w_q[:, k, (2 * h + p) * P:(2 * h + p + 1) * P],
                                                x1t[:, k, t * P:(t + 1) * P], start=(k == 0), stop=(k == KT - 1))
                last.then_inc(q_ready, 1)
                pe.wait_ge(q_copied, r + 1)
                at_least(pe, scores_read, r - SCORE_RING + 1)
                for p in range(2):
                    last = nc.tensor.matmul(score_ps[r % SCORE_RING][:, p, :], q_t[:, p, :], keys_t[:, p, :],
                                            start=True, stop=True)
                last.then_inc(scored, 1)

            pe.wait_ge(keys_in, 16)
            score(own[0])
            for head in batches[1]:
                score(head)
            for n in range(len(own)):
                following = batches[n + 2] if n + 2 < len(batches) else []
                for head in following[:2]:
                    score(head)
                if n % PEER_HEADS == 0:
                    at_least(pe, y_read, n // PEER_HEADS)
                for s in range(TOPK):
                    pe.wait_ge(diag_done, n * TOPK + s + 1)
                    pe.wait_ge(v_in[(n * TOPK + s) % V_RING], (n * TOPK + s) // V_RING * 16 + 16)
                    for c in range(2):
                        last = nc.tensor.matmul(y_ps[c][:, :], diag[:, s % DIAG_RING, :],
                                                v_rows[(n * TOPK + s) % V_RING][:, c * HALF:(c + 1) * HALF],
                                                start=(n % PEER_HEADS == 0 and s == 0),
                                                stop=(n % PEER_HEADS == PEER_HEADS - 1 and s == TOPK - 1))
                    last.then_inc(v_summed, 1)
                    if s in (3, 7) and len(following) > 2 + s // 4:
                        score(following[2 + s // 4])

        @block.scalar
        def _(act):
            def copy_queries(head):
                r = place[head]
                act.wait_ge(q_ready, r + 1)
                at_least(act, scored, r)
                nc.scalar.activation(q_t[:, :, :], q_ps[:, :, :], ACT.Copy).then_inc(q_copied, 1)

            def exponentials(n):
                t, h = own[n]
                g = n % GATES
                act.wait_ge(topped, n + 1)
                nc.scalar.activation(gate_e[:, g, :], routes["top"][:, t, h * TOPK:(h + 1) * TOPK], ACT.Exp,
                                     bias=neg_max[:, g:g + 1], accum_out=gate_z[:, g:g + 1]).then_inc(gated, 1)

            copy_queries(own[0])
            for head in batches[1]:
                copy_queries(head)
            exponentials(0)
            for n in range(len(own)):
                g = n % GATES
                following = batches[n + 2] if n + 2 < len(batches) else []
                act.wait_ge(u_read, (n + 1) * TOPK)
                nc.scalar.activation(gelu[:, g, :], dots[:, g, :], ACT.Gelu).then_inc(gelu_done, 1)
                if n + 1 < len(own):
                    exponentials(n + 1)
                if n == PEER_HEADS + 2:
                    norm.root(nc, act, 0)
                for head in following[:2]:
                    copy_queries(head)
                act.wait_ge(weighed, n + 1)
                for s in range(TOPK):
                    at_least(act, v_summed, n * TOPK + s - DIAG_RING + 1)
                    nc.scalar.activation(diag[:, s % DIAG_RING, :], ident[:, :], ACT.Copy,
                                         scale=weight[:, g, s:s + 1]).then_inc(diag_done, 1)
                    if s in (7, 11) and len(following) > 2 + (s - 4) // 4:
                        copy_queries(following[2 + (s - 4) // 4])
            act.wait_ge(lessened, 1)
            nc.scalar.activation(routes["top"][:, FIRST_TILES:TILES, :], routes["top"][:, FIRST_TILES:TILES, :],
                                 ACT.Exp).then_inc(all_exp, 1)
            norm.root(nc, act, 1)

        @block.vector
        def _(dve):
            v = nc.vector
            chain = Chain(dve, chain_sem)

            def topk(head):
                t, h = head
                r = place[head]
                top = routes["top"][:, t, h * TOPK:(h + 1) * TOPK]
                picked = (routes["picked"][:, t - TILES + DENSE_TILES, :, h * TOPK:(h + 1) * TOPK] if t in dense
                          else picked_here[:, :, :])
                dve.wait_ge(scored, r + 1)
                s_ps = score_ps[r % SCORE_RING]
                for p in range(2):
                    last = v.max(key_top[:, p, 0:8], s_ps[:, p, :])
                chain.step(last)
                for p in range(2):
                    v.max_index(key_pos[:, p, 0:8], key_top[:, p, 0:8], s_ps[:, p, :])
                for p in range(2):
                    last = v.match_replace(rest[:, p, :], key_top[:, p, 0:8], s_ps[:, p, :], NEG)
                last.then_inc(scores_read, 1)
                dve.wait_ge(scores_read, r + 1)
                for p in range(2):
                    last = v.max(key_top[:, p, 8:16], rest[:, p, :])
                chain.step(last)
                for p in range(2):
                    v.max_index(key_pos[:, p, 8:16], key_top[:, p, 8:16], rest[:, p, :])
                chain.step(v.tensor_tensor(cand[:, :, :], key_top[:, 0, :].unsqueeze(2).to_broadcast([P, TOPK, TOPK]),
                                           key_top[:, 1, :].unsqueeze(1).to_broadcast([P, TOPK, TOPK]), ALU.add))
                cand_f = cand[:, :, :].rearrange("p a b -> p (a b)")
                v.tensor_copy(key_pos_f[:, :, :], key_pos[:, :, :])
                chain.step(v.max(top[:, 0:8], cand_f))
                v.max_index(top_pos[:, 0:8], top[:, 0:8], cand_f)
                chain.step(v.match_replace(cand_rest, top[:, 0:8], cand_f, NEG))
                chain.step(v.max(top[:, 8:16], cand_rest))
                if head in own:
                    g = own.index(head) % GATES
                    at_least(dve, gated, own.index(head) - GATES + 1)
                    v.tensor_scalar(neg_max[:, g:g + 1], top[:, 0:1], -1.0, None, ALU.mult).then_inc(topped, 1)
                chain.step(v.max_index(top_pos[:, 8:16], top[:, 8:16], cand_rest))
                v.tensor_scalar(pos_half[:, 0, :], top_pos[:, :], 4, None, ALU.logical_shift_right)
                chain.step(v.tensor_scalar(pos_half[:, 1, :], top_pos[:, :], 15, None, ALU.bitwise_and))
                chain.step(v.tensor_copy(pos_half_f[:, :, :], pos_half[:, :, :]))
                for p in range(2):
                    last = v.tensor_tensor(one_hot[:, p, :, :], pos_half_f[:, p, :].unsqueeze(2).to_broadcast([P, TOPK, TOPK]),
                                           iota[:, 0:TOPK].unsqueeze(1).to_broadcast([P, TOPK, TOPK]), ALU.is_equal)
                chain.step(last)
                for p in range(2):
                    last = v.tensor_tensor(one_hot[:, p, :, :], one_hot[:, p, :, :],
                                           key_pos_f[:, p, :].unsqueeze(1).to_broadcast([P, TOPK, TOPK]), ALU.mult)
                chain.step(last)
                chain.step(v.tensor_reduce(picked, one_hot[:, :, :, :], AX.X, ALU.add))
                v.scalar_tensor_tensor(routes["expert"][:, t, h * TOPK:(h + 1) * TOPK], picked[:, 0, :], float(N_KEYS),
                                       picked[:, 1, :], ALU.mult, ALU.add).then_inc(routed, 1)

            def weigh(n):
                g = n % GATES
                dve.wait_ge(gated, n + 1)
                at_least(dve, diag_done, (n - GATES + 1) * TOPK)
                chain.step(v.reciprocal(gate_r[:, g:g + 1], gate_z[:, g:g + 1]))
                dve.wait_ge(gelu_done, n + 1)
                v.scalar_tensor_tensor(weight[:, g, :], gelu[:, g, :], gate_r[:, g:g + 1], gate_e[:, g, :],
                                       ALU.mult, ALU.mult).then_inc(weighed, 1)

            def take_sums(t):
                dve.wait_ge(v_summed, (t + 1) * SLOTS)
                for c in range(2):
                    cols = slice(c * HALF, (c + 1) * HALF)
                    last = v.scalar_tensor_tensor(x_tile[:, t, cols], x_tile[:, t, cols], DN_ALPHA, y_ps[c][:, :],
                                                  ALU.mult, ALU.add)
                last.then_inc(y_read, 1)

            def take_statistics(t):
                dve.wait_ge(y_read, t + 1)
                norm.statistics(nc, chain, t, x_tile[:, t, :])

            def finish(t):
                dve.wait_ge(ln_in, 32)
                chain.step(norm.scale(nc, dve, chain, t, x_tile[:, t, :], ln2_g))
                v.tensor_tensor(x_tile[:, t, :], x_tile[:, t, :], ln2_b[:, :], ALU.add).then_inc(normed, 1)

            topk(own[0])
            dve.wait_ge(x_in, 16)
            for n in range(len(own)):
                t, h = own[n]
                g = n % GATES
                at_least(dve, gelu_done, n - GATES + 1)
                heads = batches[n + 1]
                for s in range(TOPK):
                    dve.wait_ge(u_in[(n * TOPK + s) % U_RING], (n * TOPK + s) // U_RING * 16 + 16)
                    v.tensor_tensor_reduce(out=u_rows[(n * TOPK + s) % U_RING][:, :], in0=u_rows[(n * TOPK + s) % U_RING][:, :], in1=x_tile[:, t, :],
                                           scale=1.0, scalar=0.0, op0=ALU.mult, op1=ALU.add,
                                           accum_out=dots[:, g, s:s + 1]).then_inc(u_read, 1)
                    if s == TOPK // 2 - 1:
                        topk(heads[0])
                topk(heads[1])
                for head in heads[2:]:
                    topk(head)
                if n == PEER_HEADS:
                    take_sums(0)
                weigh(n)
                if n == PEER_HEADS + 1:
                    take_statistics(0)
                if n == PEER_HEADS + 2:
                    finish(0)
            view = routes["top"][:, FIRST_TILES:TILES, :].rearrange("p t (h s) -> p (t h) s", s=TOPK)
            sums = sum_all[:, FIRST_TILES:TILES, :].rearrange("p t h -> p (t h)")
            over = [P, (TILES - FIRST_TILES) * PEER_HEADS, TOPK]
            chain.step(v.tensor_copy(sums, view[:, :, 0]))
            v.tensor_tensor(view, view, sums.unsqueeze(2).to_broadcast(over), ALU.subtract).then_inc(lessened, 1)
            dve.wait_ge(all_exp, 1)
            chain.step(v.tensor_reduce(sums, view, AX.X, ALU.add))
            chain.step(v.reciprocal(sums, sums))
            chain.step(v.tensor_tensor(view, view, sums.unsqueeze(2).to_broadcast(over), ALU.mult))
            take_sums(FIRST_TILES - 1)
            take_statistics(FIRST_TILES - 1)
            finish(FIRST_TILES - 1)


class LayerNormBuffers:

    def __init__(self, st):
        self.stats = st.sb("ln_stats", [P, 2, 6])
        self.mean_var = st.sb("ln_mean_var", [P, 2, 2])
        self.rstd = st.sb("ln_rstd", [P, 2, 2])
        self.var_ready, self.rooted = st.sem("ln_var_ready"), st.sem("ln_rooted")

    def root(self, nc, act, i):
        act.wait_ge(self.var_ready, i + 1)
        nc.scalar.activation(self.rstd[:, i % 2, 1:2], self.rstd[:, i % 2, 0:1], ACT.Sqrt).then_inc(self.rooted, 1)

    def statistics(self, nc, chain, i, rows):
        v = nc.vector
        for c in range(2):
            last = v.bn_stats(self.stats[:, c, :], rows[:, c * HALF:(c + 1) * HALF])
        chain.step(last)
        chain.step(v.bn_aggr(self.mean_var[:, i % 2, :], self.stats[:, :, :].rearrange("p a b -> p (a b)")))
        v.tensor_scalar(self.rstd[:, i % 2, 0:1], self.mean_var[:, i % 2, 1:2], LN_EPS, None, ALU.add).then_inc(self.var_ready, 1)

    def scale(self, nc, dve, chain, i, rows, gain):
        v = nc.vector
        dve.wait_ge(self.rooted, i + 1)
        chain.step(v.reciprocal(self.rstd[:, i % 2, 0:1], self.rstd[:, i % 2, 1:2]))
        chain.step(v.tensor_scalar(rows, rows, self.mean_var[:, i % 2, 0:1], self.rstd[:, i % 2, 0:1],
                                   ALU.subtract, ALU.mult))
        return v.tensor_tensor(rows, rows, gain[:, :], ALU.mult)


def shared_routes(nc, ctx):
    return {
        "expert": ctx.enter_context(nc.sbuf_tensor("route_expert", [P, TILES, SLOTS], U32)),
        "top": ctx.enter_context(nc.sbuf_tensor("route_top", [P, TILES, SLOTS], F32)),
        "picked": ctx.enter_context(nc.sbuf_tensor("route_picked", [P, DENSE_TILES, 2, SLOTS], F32)),
    }


STREAMS = 6
PER_ROUND = 18
TOGETHER = 4
G_COLS = 64
assert (PEER_HEADS - 1) * PER_ROUND <= N_KEYS and PER_ROUND % STREAMS == 0 and PER_ROUND % 2 == 0


def experts_stage(nc, st, consts, x1t, routes, dram, x1_rows, gates_dram, out_rows):
    ident, iota = consts["ident"], consts["iota"]
    RING = 6
    U_PER_ROUND = MID_TILES * TOPK // RING
    assert U_PER_ROUND * RING == MID_TILES * TOPK
    MID_ROUND = MID_TILES * TOPK
    GROUPS = N_DENSE // TOGETHER
    STORE_GROUPS = G_COLS // TOGETHER
    G_STORES = N_DENSE // G_COLS

    x_mid = st.sb("x_mid", [P, MID_TILES, D_MODEL])
    acc = st.sb("acc", [P, MID_TILES, D_MODEL])
    u_rows = [st.sb(f"u_rows{r}", [P, D_MODEL]) for r in range(RING)]
    v_rows = [st.sb(f"v_rows{r}", [P, D_MODEL]) for r in range(RING)]
    expert_now = [st.sb(f"expert_now{m}", [P, TOPK], U32) for m in range(MID_TILES)]
    gate_now = st.sb("gate_now", [P, MID_TILES, TOPK])
    dots = st.sb("dots", [P, MID_TILES, TOPK])
    gelu_mid = st.sb("gelu_mid", [P, MID_TILES, TOPK])
    weight = st.sb("weight", [P, MID_TILES, TOPK])
    by_slot = st.sb("by_slot", [P, DENSE_TILES, 3, P])
    hot = [st.sb(f"hot{r}", [P, 2, TOGETHER * N_KEYS]) for r in range(2)]
    g_build = [st.sb(f"g_build{r}", [P, N_KEYS, G_COLS]) for r in range(2)]
    flat = [b[:, :, :].rearrange("p a b -> p (a b)") for b in g_build]
    half = STREAMS // 2
    G_AT = half * 2 * D_MODEL
    GELU_AT = G_AT + 2 * N_DENSE

    def part(e, at, width):
        r = e % STREAMS
        start = (r % half) * 2 * D_MODEL + at
        return flat[r // half][:, start:start + width]

    def g_pair(e):
        start = (G_AT, G_AT, GELU_AT + N_DENSE)[e % STREAMS // 2]
        return flat[e % STREAMS // 2 % 2][:, start:start + 2 * N_DENSE].rearrange("p (b c) -> p b c", b=G_STORES)

    def u_e(e, k):
        return part(e, k * P, P)

    def v_e(e, c):
        return part(e, D_MODEL + c * HALF, HALF)

    def g_e(e):
        return g_pair(e)[:, :, (e % 2) * G_COLS:(e % 2 + 1) * G_COLS]

    gelu_e = [f[:, GELU_AT:GELU_AT + N_DENSE] for f in flat]
    assert GELU_AT + 3 * N_DENSE <= N_KEYS * G_COLS
    weighed_e = [st.sb(f"weighed_e{r}", [P, N_DENSE]) for r in range(2)]
    zero = st.sb("zero", [P, P])
    norm = LayerNormBuffers(st)

    h_ps = [st.ps(f"h_ps{r}", [P, HALF]) for r in range(2)]
    y_ps = [[st.ps(f"y_ps{t}{c}", [P, HALF]) for c in range(2)] for t in range(DENSE_TILES)]

    x_in, tail_in = st.sem("x_in"), st.sem("tail_in")
    u_in = [st.sem(f"u_in{r}") for r in range(RING)]
    v_in = [st.sem(f"v_in{r}") for r in range(RING)]
    staged = st.sem("staged")
    u_read = st.sem("u_read")
    gelu_ready = st.sem("gelu_ready")
    weighed = st.sem("weighed")
    v_read = st.sem("v_read")
    turned, turned_out = st.sem("turned"), st.sem("turned_out")
    hot_set = st.sem("hot_set")
    hot_ready = st.sem("hot_ready")
    g_made = st.sem("g_made")
    g_out = st.sem("g_out")
    g_stored = [st.sem(f"g_stored{r}") for r in range(2)]
    e_in = [st.sem(f"e_in{r}") for r in range(STREAMS)]
    h_done = st.sem("h_done")
    gelu_done = st.sem("gelu_done")
    w_done = st.sem("w_done")
    y_done = st.sem("y_done")
    scaled = st.sem("scaled")
    normed, stored, chain_sem = st.sem("normed"), st.sem("stored"), st.sem("chain")
    pool_passed = st.sem("pool_passed")

    def number(h, e):
        return (h - 1) * PER_ROUND + e

    TAIL = [(PEER_HEADS, e) for e in range(N_KEYS - (PEER_HEADS - 1) * PER_ROUND)]

    last_rows = [acc[:, m, :] for m in range(MID_TILES)] + [u_rows[k][:, :] for k in range(DENSE_TILES)]
    gain, offset = (b[:, :, :].rearrange("p a b -> p (a b)") for b in hot)

    with nc.Block() as block:
        @block.sync
        def _(sp):
            for m in range(MID_TILES):
                t = FIRST_TILES + m
                sp.dma_start(x_mid[:, m, :], x1_rows[t * P:(t + 1) * P, :]).then_inc(x_in, 16)
            g_view = gates_dram.rearrange("(b r i) c -> b i r c", b=G_STORES, i=N_KEYS)
            for b in range(G_STORES):
                sp.wait_ge(g_out, (b + 1) * STORE_GROUPS)
                sp.dma_start(g_view[b, :, :, :], g_build[b % 2][:, :, :].rearrange("p (r j) t -> p r (j t)", j=2)).then_inc(g_stored[b % 2], 16)
            for r in range(2):
                sp.wait_ge(g_stored[r], 16 * G_STORES // 2)
            v_view = dram["v"].rearrange("(i j) d -> i (j d)", j=N_KEYS)

            g_pairs = gates_dram.rearrange("(b r) c -> r b c", b=G_STORES)

            def load(h, e):
                j = number(h, e)
                sp.wait_ge(y_done, j + 1)
                if e % 2 == 1:
                    sp.dma_start(g_pair(e), g_pairs[bass.ds((j - 1) * (P // 2), P), :, :]).then_inc(e_in[(e - 1) % STREAMS], 16)
                sp.dma_start(part(e, 0, D_MODEL), dram["u_t"][bass.ds(j * P, P), :]).then_inc(e_in[e % STREAMS], 16)
                sp.dma_start(part(e, D_MODEL, D_MODEL), v_view[:, bass.ds(j * D_MODEL, D_MODEL)]).then_inc(e_in[e % STREAMS], 16)

            with sp.Fori(1, PEER_HEADS) as h:
                for e in range(PER_ROUND):
                    load(h, e)
            for h, e in TAIL:
                load(h, e)
            sp.wait_ge(g_made, GROUPS)
            sp.dma_start(hot[0][:, :, :].rearrange("p a b -> p (a b)"), dram["ln2_g"].partition_broadcast(P)).then_inc(tail_in, 16)
            sp.dma_start(hot[1][:, :, :].rearrange("p a b -> p (a b)"), dram["ln2_b"].partition_broadcast(P)).then_inc(tail_in, 16)
            sp.wait_ge(u_read, PEER_HEADS * MID_ROUND)
            for k in range(DENSE_TILES):
                t = TILES - DENSE_TILES + k
                sp.dma_start(u_rows[k][:, :], x1_rows[t * P:(t + 1) * P, :]).then_inc(tail_in, 16)
            for k in range(MID_TILES + DENSE_TILES):
                t = FIRST_TILES + k
                sp.wait_ge(normed, k + 1)
                sp.dma_start(out_rows[t * P:(t + 1) * P, :], last_rows[k]).then_inc(stored, 16)
            sp.wait_ge(stored, 16 * (MID_TILES + DENSE_TILES))

        @block.gpsimd
        def _(pool):
            def gather(h, m, s, rows, landed, table, free):
                q = m * TOPK + s
                at_least(pool, free, h * MID_ROUND + q - RING + 1)
                pool.sem_inc(pool_passed, 1)
                nc.gpsimd.indirect_dma_start(
                    rows[q % RING][:, :], None, table,
                    bass.IndirectOffsetOnAxis(ap=expert_now[m][:, s:s + 1], axis=0)).then_inc(landed[q % RING], 16)

            def gather_u(h, m):
                pool.wait_ge(staged, h * MID_TILES + m + 1)
                for s in range(TOPK):
                    gather(h, m, s, u_rows, u_in, dram["u"], u_read)

            def gather_v(h, m):
                for s in range(TOPK):
                    gather(h, m, s, v_rows, v_in, dram["v"], v_read)

            def head_program(h, first, last):
                for m in range(MID_TILES):
                    if m + 1 < MID_TILES:
                        gather_u(h, m + 1)
                    elif not last:
                        gather_u(h + 1, 0)
                    gather_v(h, m)

            gather_u(0, 0)
            head_program(0, True, False)
            with pool.Fori(1, PEER_HEADS - 1) as h:
                head_program(h, False, False)
            head_program(PEER_HEADS - 1, False, True)
            for k in range(MID_TILES + DENSE_TILES):
                pool.wait_ge(scaled, k + 1)
                nc.gpsimd.tensor_tensor(last_rows[k], last_rows[k], offset, ALU.add).then_inc(normed, 1)

        @block.tensor
        def _(pe):
            for k in range(DENSE_TILES):
                at_least(pe, turned_out, k - 1)
                for c in range(3):
                    what = routes["picked"][:, k, c, :] if c < 2 else routes["top"][:, TILES - DENSE_TILES + k, :]
                    last = nc.tensor.transpose(h_ps[k % 2][:, c * P:(c + 1) * P], what, ident[:, :])
                last.then_inc(turned, 1)
            for n in range(GROUPS):
                pe.wait_ge(hot_ready, n + 1)
                if n < 2:
                    pe.wait_ge(turned_out, DENSE_TILES)
                at_least(pe, g_out, n - 1)
                for i in range(TOGETHER):
                    at = slice(i * N_KEYS, (i + 1) * N_KEYS)
                    last = nc.tensor.matmul(h_ps[n % 2][:, at], hot[n % 2][:, 0, at], hot[n % 2][:, 1, at],
                                            start=True, stop=True)
                last.then_inc(g_made, 1)
            for t in range(DENSE_TILES):
                for c in range(2):
                    nc.tensor.matmul(y_ps[t][c][:, :], zero[:, :], x1t[:, c, 0:HALF], start=True, stop=False)
            pe.wait_ge(g_out, GROUPS)
            pe.sem_inc(y_done, STREAMS)

            def product_h(h, e):
                j = number(h, e)
                use = (h - 1) * (PER_ROUND // STREAMS) + e // STREAMS + 1
                pe.wait_ge(e_in[e % STREAMS], use * (48 if e % 2 == 0 else 32))
                pe.wait_ge(gelu_done, j + 1)
                for k in range(KT):
                    last = nc.tensor.matmul(h_ps[e % 2][:, 0:N_DENSE], u_e(e, k), x1t[:, k, DENSE_START:SEQ],
                                            start=(k == 0), stop=(k == KT - 1))
                last.then_inc(h_done, 1)

            def product_y(h, e, final=False):
                pe.wait_ge(w_done, number(h, e) + 3)
                for t in range(DENSE_TILES):
                    for c in range(2):
                        last = nc.tensor.matmul(y_ps[t][c][:, :], weighed_e[e % 2][:, t * P:(t + 1) * P], v_e(e, c),
                                                start=False, stop=final)
                last.then_inc(y_done, 1)

            product_h(1, 0)
            with pe.Fori(1, PEER_HEADS) as h:
                for e in range(PER_ROUND):
                    if e + 1 < PER_ROUND:
                        product_h(h, e + 1)
                    else:
                        product_h(h + 1, 0)
                    product_y(h, e)
            for h, e in TAIL:
                if (h, e + 1) in TAIL:
                    product_h(h, e + 1)
                product_y(h, e, (h, e) == TAIL[-1])

        @block.scalar
        def _(act):
            for k in range(DENSE_TILES):
                act.wait_ge(turned, k + 1)
                nc.scalar.activation(by_slot[:, k, :, :], h_ps[k % 2][:, 0:3 * P].rearrange("p (c t) -> p c t", c=3),
                                     ACT.Copy).then_inc(turned_out, 1)
            act.sem_inc(gelu_done, 2)

            def scale_rows(n):
                act.wait_ge(hot_set, n + 1)
                k, t = n * TOGETHER // P, n * TOGETHER % P
                for i in range(TOGETHER):
                    row = hot[n % 2][:, 1, i * N_KEYS:(i + 1) * N_KEYS]
                    last = nc.scalar.activation(row, row, ACT.Copy, scale=by_slot[:, k, 2, t + i:t + i + 1])
                last.then_inc(hot_ready, 1)

            def take_gates(n):
                b = n // STORE_GROUPS
                act.wait_ge(g_made, n + 1)
                at_least(act, g_stored[b % 2], 16 * (b // 2))
                at = (n % STORE_GROUPS) * TOGETHER
                nc.scalar.activation(g_build[b % 2][:, :, at:at + TOGETHER],
                                     h_ps[n % 2][:, :].rearrange("p (t j) -> p j t", t=TOGETHER),
                                     ACT.Copy).then_inc(g_out, 1)

            def gelu_unit(h, m):
                n = h * MID_TILES + m
                act.wait_ge(u_read, (n + 1) * TOPK)
                at_least(act, weighed, n - MID_TILES + 1)
                nc.scalar.activation(gelu_mid[:, m, :], dots[:, m, :], ACT.Gelu).then_inc(gelu_ready, 1)

            def gelu_h(h, e):
                j = number(h, e)
                act.wait_ge(h_done, j + 1)
                act.wait_ge(w_done, j + 1)
                nc.scalar.activation(gelu_e[e % 2], h_ps[e % 2][:, 0:N_DENSE], ACT.Gelu).then_inc(gelu_done, 1)

            per_unit = GROUPS // MID_TILES
            act.wait_ge(turned_out, DENSE_TILES)
            for m in range(MID_TILES):
                for i in range(per_unit):
                    scale_rows(m * per_unit + i)
                    if m + i > 0:
                        take_gates(m * per_unit + i - 1)
                    if i == per_unit // 2:
                        gelu_unit(0, m)
            take_gates(GROUPS - 1)
            with act.Fori(1, PEER_HEADS) as h:
                for e in range(PER_ROUND):
                    gelu_h(h, e)
                    if e % (PER_ROUND // MID_TILES) == PER_ROUND // MID_TILES // 2 - 1:
                        gelu_unit(h, e // (PER_ROUND // MID_TILES))
            for h, e in TAIL:
                gelu_h(h, e)
            for k in range(MID_TILES + DENSE_TILES):
                norm.root(nc, act, k)

        @block.vector
        def _(dve):
            v = nc.vector
            chain = Chain(dve, chain_sem)
            chain.step(v.memset(zero[:, :], 0.0))
            chain.step(v.memset(acc[:, :, :], 0.0))
            dve.sem_inc(w_done, 2)

            def stage(h, m):
                t = FIRST_TILES + m
                v.tensor_copy(gate_now[:, m, :], routes["top"][:, t, bass.ds(h * TOPK, TOPK)])
                v.tensor_copy(expert_now[m][:, :], routes["expert"][:, t, bass.ds(h * TOPK, TOPK)]).then_inc(staged, 1)

            def one_hots(n):
                at_least(dve, g_made, n - 1)
                k, t = n * TOGETHER // P, n * TOGETHER % P
                over = [P, 2, TOGETHER, N_KEYS]
                v.tensor_tensor(hot[n % 2][:, :, :].rearrange("p c (t j) -> p c t j", t=TOGETHER),
                                iota[:, :].unsqueeze(1).unsqueeze(1).to_broadcast(over),
                                by_slot[:, k, 0:2, t:t + TOGETHER].unsqueeze(3).to_broadcast(over),
                                ALU.is_equal).then_inc(hot_set, 1)

            def in_blocks(ap):
                return ap.rearrange("p (b t) -> p b t", b=G_STORES)

            def weigh_e(h, e):
                j = number(h, e)
                dve.wait_ge(gelu_done, j + 3)
                dve.wait_ge(y_done, j + STREAMS - 1)
                v.tensor_tensor(in_blocks(weighed_e[e % 2][:, :]), in_blocks(gelu_e[e % 2]), g_e(e), ALU.mult).then_inc(w_done, 1)

            def dot(h, m, s):
                q = m * TOPK + s
                use = h * U_PER_ROUND + q // RING + 1
                dve.wait_ge(u_in[q % RING], use * 16)
                v.tensor_tensor_reduce(out=u_rows[q % RING][:, :], in0=u_rows[q % RING][:, :], in1=x_mid[:, m, :],
                                       scale=1.0, scalar=0.0, op0=ALU.mult, op1=ALU.add,
                                       accum_out=dots[:, m, s:s + 1]).then_inc(u_read, 1)

            def add_v(h, m, s):
                q = m * TOPK + s
                use = h * U_PER_ROUND + q // RING + 1
                dve.wait_ge(v_in[q % RING], use * 16)
                at_least(dve, v_read, h * MID_ROUND + q)
                v.scalar_tensor_tensor(acc[:, m, :], v_rows[q % RING][:, :], weight[:, m, s:s + 1],
                                       acc[:, m, :], ALU.mult, ALU.add).then_inc(v_read, 1)

            def unit(h, m, last, beside):
                n = h * MID_TILES + m
                at_least(dve, gelu_ready, n - MID_TILES + 1)
                for s in range(TOPK):
                    dot(h, m, s)
                    beside(s)
                before = (h, m - 1) if m > 0 else (h - 1, MID_TILES - 1)
                if not (isinstance(h, int) and h == 0 and m == 0):
                    dve.wait_ge(weighed, n)
                for s in range(TOPK):
                    if not (isinstance(h, int) and h == 0 and m == 0):
                        add_v(*before, s)
                    beside(TOPK + s)
                dve.wait_ge(gelu_ready, n + 1)
                v.tensor_tensor(weight[:, m, :], gelu_mid[:, m, :], gate_now[:, m, :], ALU.mult).then_inc(weighed, 1)
                after = (h, m + 2) if m + 2 < MID_TILES else (h + 1, m + 2 - MID_TILES)
                if not (last and m + 2 >= MID_TILES):
                    stage(*after)

            def head_program(h, last):
                each = PER_ROUND // MID_TILES
                every = 2 * TOPK // each
                for m in range(MID_TILES):
                    def beside(i, m=m):
                        if i % every == every // 2 and i // every < each:
                            weigh_e(h, m * each + i // every)
                    unit(h, m, last, beside)

            stage(0, 0)
            stage(0, 1)
            dve.wait_ge(x_in, 16 * MID_TILES)
            dve.wait_ge(turned_out, DENSE_TILES)
            dve.wait_ge(staged, 2)
            for m in range(MID_TILES):
                unit(0, m, False, lambda i, m=m: one_hots(m * 2 * TOPK + i))
            with dve.Fori(1, PEER_HEADS - 1) as h:
                head_program(h, False)
            head_program(PEER_HEADS - 1, True)
            dve.wait_ge(weighed, PEER_HEADS * MID_TILES)
            for s in range(TOPK):
                add_v(PEER_HEADS - 1, MID_TILES - 1, s)
                if s % 8 == 4 and s // 8 < len(TAIL):
                    weigh_e(*TAIL[s // 8])

            dve.wait_ge(v_read, PEER_HEADS * MID_ROUND)
            dve.wait_ge(tail_in, 16 * (DENSE_TILES + 2))
            for k in range(MID_TILES + DENSE_TILES):
                if k < MID_TILES:
                    chain.step(v.scalar_tensor_tensor(acc[:, k, :], x_mid[:, k, :], DN_ALPHA, acc[:, k, :], ALU.mult, ALU.add))
                else:
                    if k == MID_TILES:
                        dve.wait_ge(y_done, N_KEYS + STREAMS)
                    for c in range(2):
                        cols = slice(c * HALF, (c + 1) * HALF)
                        last = v.scalar_tensor_tensor(last_rows[k][:, cols], last_rows[k][:, cols], DN_ALPHA,
                                                      y_ps[k - MID_TILES][c][:, :], ALU.mult, ALU.add)
                    chain.step(last)
                norm.statistics(nc, chain, k, last_rows[k])
                if k > 0:
                    norm.scale(nc, dve, chain, k - 1, last_rows[k - 1], gain).then_inc(scaled, 1)
            k = MID_TILES + DENSE_TILES - 1
            norm.scale(nc, dve, chain, k, last_rows[k], gain).then_inc(scaled, 1)



DA_HEADS = 4
DA_DIM = 64
ROPE_HALF = 8
ROPE_THETA = 500000.0
BIG = 1.0e30
ML_HEADS = 4
ML_DIM = 128
CONV = 5
PAD = (CONV - 1) // 2
LAMBDA_INIT = 0.8 - 0.6 * math.exp(0.0)
WIDTH = 512
COL_DA_Q, COL_DA_K, COL_DA_V, COL_ML_Q, COL_ML_K, COL_ML_V, COL_ML_O = (WIDTH * i for i in range(7))
COL_GATES = 7 * WIDTH
COL_BRANCH = COL_GATES + 4 * ML_HEADS


class Stage:

    def __init__(self, nc, ctx, name):
        self.nc, self.ctx, self.name, self.sems = nc, ctx, name, []
        ctx.callback(self.clear)

    def clear(self):
        if self.sems:
            self.nc.clear_and_free_semaphores(self.sems)
            self.nc.all_engine_barrier()

    def sb(self, name, shape, dt=F32):
        return self.ctx.enter_context(self.nc.sbuf_tensor(f"{self.name}_{name}", shape, dt))

    def ps(self, name, shape, dt=F32):
        return self.ctx.enter_context(self.nc.psum_tensor(f"{self.name}_{name}", shape, dt))

    def sem(self, name):
        self.sems.append(self.nc.alloc_semaphore(name=f"{self.name}_{name}"))
        return self.sems[-1]


def project_stage(nc, st, consts, x_t, ml, qkv, dram):
    ident = consts["ident"]
    w = [st.sb(f"w{r}", [P, KT, WIDTH]) for r in range(2)]
    w_gates = st.sb("w_gates", [P, KT, 16])
    gate_b = st.sb("gate_b", [P, 16])
    conv_w = st.sb("conv_w", [P, 2 * ML_HEADS, CONV])
    conv_b = st.sb("conv_b", [P, 2 * ML_HEADS])
    x_pad = [st.sb(f"x_pad{r}", [P, SEQ + 2 * PAD]) for r in range(2)]
    ROT = 3
    rot = [st.sb(f"rot{r}", [P, WIDTH]) for r in range(ROT)]
    turned = st.sb("turned", [P, 4, 8, ROPE_HALF])
    log_tmp = st.sb("log_tmp", [P, 3, TILES, 2, ML_HEADS])
    forget = ml["gates"][:, :, :].rearrange("p t (d k h) -> p t d k h", d=2, k=2)[:, :, :, 1, :]
    banks = [st.ps(f"bank{r}", [P, WIDTH]) for r in range(8)]

    small_in, w_first = st.sem("small_in"), st.sem("w_first")
    x_in = [st.sem(f"x_in{half}") for half in range(2)]
    w_in = [st.sem(f"w_in{r}") for r in range(2)]
    pads_set = st.sem("pads_set")
    filled = st.sem("filled")
    act_copied = st.sem("act_copied")
    dve_copied = st.sem("dve_copied")
    padded = st.sem("padded")
    convolved = st.sem("convolved")
    rotated = st.sem("rotated")
    exp_done, ln_done, absf_done = st.sem("exp_done"), st.sem("ln_done"), st.sem("absf_done")
    silu_done = st.sem("silu_done")
    chain_sem = st.sem("chain")

    units = []
    for g in range(2):
        for c in range(4):
            units += [("conv", (g * 4 + c, half), "act") for half in range(2)]
    units.append(("gates", None, "dve"))
    turns = []
    for g in range(2):
        for t in range(TILES):
            units.append(("rope", (g, t), "act"))
            turns.append((g, t))
            if len(turns) > 2:
                units.append(("turn", turns.pop(0), "dve"))
    units += [("turn", turn, "dve") for turn in turns]
    units += [("v", t, "act") for t in range(TILES)]
    units += [("ml_v", t, "dve") for t in range(TILES)]
    units += [("ml_o", t, "act") for t in range(TILES)]
    blocks = [COL_ML_Q, COL_ML_K, COL_DA_Q, COL_DA_K, COL_DA_V, COL_ML_V, COL_ML_O]

    def block_of(kind, which):
        return {"conv": lambda: which[0] // 4, "rope": lambda: 2 + which[0], "v": lambda: 4,
                "ml_v": lambda: 5, "ml_o": lambda: 6}.get(kind, lambda: None)()

    last_of_block = {}
    for i, (kind, which, _) in enumerate(units):
        if block_of(kind, which) is not None:
            last_of_block[block_of(kind, which)] = i
    rope_order = [which for kind, which, _ in units if kind == "rope"]

    def emptied(i):
        return sum(e == units[i][2] for _, _, e in units[:i + 1])

    with nc.Block() as block:
        @block.sync
        def _(sp):
            w_view = dram["w_in"].rearrange("(k p) n -> p k n", p=P)
            sp.dma_start(w[0][:, :, 0:P], w_view[:, :, blocks[0]:blocks[0] + P]).then_inc(w_first, 16)
            for half in range(2):
                cols = slice(half * WIDTH, (half + 1) * WIDTH)
                for k in range(KT):
                    sp.dma_start(x_t[:, k, cols], dram["x_t"][k * P:(k + 1) * P, cols]).then_inc(x_in[half], 16)
            sp.dma_start(w[0][:, :, P:WIDTH], w_view[:, :, blocks[0] + P:blocks[0] + WIDTH]).then_inc(w_in[0], 16)
            sp.dma_start(w_gates[:, :, :], w_view[:, :, COL_GATES:COL_GATES + 16]).then_inc(small_in, 16)
            sp.dma_start(gate_b[:, :], dram["gate_b"].partition_broadcast(P)).then_inc(small_in, 16)
            sp.dma_start(conv_w[:, :, :], dram["conv_w"]).then_inc(small_in, 16)
            sp.dma_start(conv_b[:, :], dram["conv_b"]).then_inc(small_in, 16)
            for name in ("ident", "iota", "cos", "sin", "mask", "pick"):
                sp.dma_start(consts[name][tuple(slice(None) for _ in consts[name].shape)], dram[name]).then_inc(small_in, 16)
            for i, col in enumerate(blocks):
                if i == 0:
                    continue
                if i >= 2:
                    sp.wait_ge(filled, last_of_block[i - 2] + 1)
                sp.dma_start(w[i % 2][:, :, :], w_view[:, :, col:col + WIDTH]).then_inc(w_in[i % 2], 16)

        @block.gpsimd
        def _(pool):
            for r in range(2):
                nc.gpsimd.memset(x_pad[r][:, 0:PAD], 0.0)
                nc.gpsimd.memset(x_pad[r][:, SEQ + PAD:SEQ + 2 * PAD], 0.0).then_inc(pads_set, 1)
            nc.gpsimd.memset(ml["v"][:, :, :, ML_DIM:ML_DIM + 1], 1.0).then_inc(pads_set, 1)
            pool.wait_ge(pads_set, 3)

        SMALL = 16 * 10

        @block.tensor
        def _(pe):
            pe.wait_ge(w_first, 16)
            started = set()
            for i, (kind, which, engine) in enumerate(units):
                bank = banks[i % 8]
                if i >= 8:
                    pe.wait_ge(act_copied if units[i - 8][2] == "act" else dve_copied, emptied(i - 8))
                b = block_of(kind, which)
                if kind == "conv" and which[0] == 0:
                    pe.wait_ge(x_in[which[1]], 16 * KT)
                elif b is not None and b not in started:
                    started.add(b)
                    pe.wait_ge(w_in[b % 2], 16 * (b // 2 + 1))
                for k in range(KT):
                    flags = dict(start=(k == 0), stop=(k == KT - 1))
                    if kind == "conv":
                        c, half = which
                        last = nc.tensor.matmul(bank[:, :], w[b % 2][:, k, (c % 4) * P:(c % 4 + 1) * P],
                                                x_t[:, k, half * WIDTH:(half + 1) * WIDTH], **flags)
                    elif kind in ("rope", "v", "ml_v", "ml_o"):
                        t = which[1] if kind == "rope" else which
                        last = nc.tensor.matmul(bank[:, :], x_t[:, k, t * P:(t + 1) * P], w[b % 2][:, k, :], **flags)
                if kind == "gates":
                    pe.wait_ge(small_in, SMALL)
                    for t in range(TILES):
                        for k in range(KT):
                            last = nc.tensor.matmul(bank[:, t * 16:(t + 1) * 16], x_t[:, k, t * P:(t + 1) * P],
                                                    w_gates[:, k, :], start=(k == 0), stop=(k == KT - 1))
                if kind == "turn":
                    n = rope_order.index(which)
                    pe.wait_ge(rotated, n + 1)
                    for c in range(4):
                        last = nc.tensor.transpose(bank[:, c * P:(c + 1) * P], rot[n % ROT][:, c * P:(c + 1) * P], ident[:, :])
                last.then_inc(filled, 1)

        def full(bank, parts):
            return bank[:, :].rearrange("p (a b) -> p a b", a=parts)

        @block.scalar
        def _(act):
            silus = 0

            def silu(c):
                act.wait_ge(convolved, c + 1)
                dst = (ml["q_t"] if c < 4 else ml["k_t"])[:, c % 4, :]
                nc.scalar.activation(dst, dst, ACT.Silu).then_inc(silu_done, 1)

            act.wait_ge(small_in, SMALL)
            for i, (kind, which, engine) in enumerate(units):
                if kind == "gates":
                    act.wait_ge(absf_done, 1)
                    nc.scalar.activation(log_tmp[:, 1, :, :, :], log_tmp[:, 0, :, :, :], ACT.Exp).then_inc(exp_done, 1)
                    act.wait_ge(exp_done, 1)
                    nc.scalar.activation(log_tmp[:, 2, :, :, :], log_tmp[:, 1, :, :, :], ACT.Ln, bias=1.0).then_inc(ln_done, 1)
                if engine != "act":
                    continue
                bank = banks[i % 8]
                act.wait_ge(filled, i + 1)
                if kind == "conv":
                    c, half = which
                    if c >= 2:
                        act.wait_ge(convolved, c - 1)
                    nc.scalar.activation(x_pad[c % 2][:, PAD + half * WIDTH:PAD + (half + 1) * WIDTH], bank[:, :],
                                         ACT.Copy).then_inc(act_copied, 1)
                elif kind == "rope":
                    n = rope_order.index(which)
                    if n >= ROT:
                        turned_unit = units.index(("turn", rope_order[n - ROT], "dve"))
                        act.wait_ge(filled, turned_unit + 1)
                    nc.scalar.activation(rot[n % ROT][:, :], bank[:, :], ACT.Copy).then_inc(act_copied, 1)
                elif kind == "v":
                    nc.scalar.activation(qkv["v"][:, which, :], bank[:, :], ACT.Copy).then_inc(act_copied, 1)
                elif kind == "ml_o":
                    nc.scalar.activation(ml["o"][:, which, :], bank[:, :], ACT.Sigmoid).then_inc(act_copied, 1)
                if kind == "v":
                    silu(silus)
                    silus += 1
            act.wait_ge(silu_done, 2 * ML_HEADS)

        @block.vector
        def _(dve):
            v = nc.vector
            chain = Chain(dve, chain_sem)
            acts = {i: emptied(i) for i, u in enumerate(units) if u[2] == "act"}
            dve.wait_ge(small_in, SMALL)
            dve.wait_ge(pads_set, 3)
            for i, (kind, which, engine) in enumerate(units):
                bank = banks[i % 8]
                if kind == "conv" and which[1] == 1:
                    c = which[0]
                    dve.wait_ge(act_copied, acts[i])
                    y = (ml["q_t"] if c < 4 else ml["k_t"])[:, c % 4, :]
                    row = x_pad[c % 2]
                    chain.step(v.tensor_scalar(y, row[:, 0:SEQ], conv_w[:, c, 0:1], conv_b[:, c:c + 1], ALU.mult, ALU.add))
                    for tap in range(1, CONV):
                        step = v.scalar_tensor_tensor(y, row[:, tap:tap + SEQ], conv_w[:, c, tap:tap + 1], y, ALU.mult, ALU.add)
                        if tap < CONV - 1:
                            chain.step(step)
                    step.then_inc(convolved, 1)
                if kind == "rope":
                    n = rope_order.index(which)
                    dve.wait_ge(act_copied, acts[i])
                    q = rot[n % ROT][:, :].rearrange("p (g d) -> p g d", d=DA_DIM)
                    low, high = q[:, :, 0:ROPE_HALF], q[:, :, ROPE_HALF:2 * ROPE_HALF]
                    cos = consts["cos"][:, which[1], :].unsqueeze(1).to_broadcast([P, 8, ROPE_HALF])
                    sin = consts["sin"][:, which[1], :].unsqueeze(1).to_broadcast([P, 8, ROPE_HALF])
                    for j, (a, b) in enumerate(((low, cos), (high, sin), (high, cos), (low, sin))):
                        last = v.tensor_tensor(turned[:, j, :, :], a, b, ALU.mult)
                    chain.step(last)
                    v.tensor_tensor(low, turned[:, 0, :, :], turned[:, 1, :, :], ALU.subtract)
                    v.tensor_tensor(high, turned[:, 2, :, :], turned[:, 3, :, :], ALU.add).then_inc(rotated, 1)
                    dve.wait_ge(rotated, n + 1)
                if engine != "dve":
                    continue
                dve.wait_ge(filled, i + 1)
                if kind == "gates":
                    v.tensor_tensor(ml["gates"][:, :, :], bank[:, 0:TILES * 16].rearrange("p (t g) -> p t g", g=16),
                                    gate_b[:, :].unsqueeze(1).to_broadcast([P, TILES, 16]), ALU.add).then_inc(dve_copied, 1)
                    dve.wait_ge(dve_copied, emptied(i))
                    chain.step(v.tensor_scalar(log_tmp[:, 0, :, :, :], forget, -1.0, None, ALU.mult))
                    v.tensor_tensor(log_tmp[:, 0, :, :, :], log_tmp[:, 0, :, :, :], forget, ALU.min).then_inc(absf_done, 1)
                elif kind == "turn":
                    g, t = which
                    v.tensor_copy((qkv["q_t"] if g == 0 else qkv["k_t"])[:, :, t * P:(t + 1) * P], full(bank, 4)).then_inc(dve_copied, 1)
                elif kind == "ml_v":
                    v.tensor_copy(ml["v"][:, which, :, 0:ML_DIM], full(bank, 4)).then_inc(dve_copied, 1)
            dve.wait_ge(ln_done, 1)
            chain.step(v.scalar_tensor_tensor(forget, forget, 0.0, log_tmp[:, 2, :, :, :], ALU.min, ALU.subtract))


def attention_stage(nc, st, consts, qkv, y_t, dram):
    ident = consts["ident"]
    SCORES, PROBS = 3, 4
    prob = [st.sb(f"prob{r}", [P, SEQ]) for r in range(PROBS)]
    diff_t = st.sb("diff_t", [P, TILES, P])
    o = st.sb("o", [P, TILES, DA_HEADS, P])
    square = st.sb("square", [P, P])
    sum_sq = st.sb("sum_sq", [P, TILES, DA_HEADS])
    rstd = st.sb("rstd", [P, 2, TILES, DA_HEADS])
    lam_in = st.sb("lam_in", [P, 4, DA_DIM])
    lam_prod = st.sb("lam_prod", [P, 2, DA_DIM])
    lam = st.sb("lam", [P, 4])
    subln = st.sb("subln", [P, 2])
    top = st.sb("top", [P, PROBS])
    neg = st.sb("neg", [P, PROBS])
    z = st.sb("z", [P, PROBS])
    rz = st.sb("rz", [P, PROBS])
    score = [st.ps(f"score{r}", [P, SEQ]) for r in range(SCORES)]
    turn_ps = st.ps("turn_ps", [P, 4, P])
    o_ps = st.ps("o_ps", [P, WIDTH])

    small_in, lam_sum, lam_exp = st.sem("small_in"), st.sem("lam_sum"), st.sem("lam_exp")
    scored = st.sem("scored")
    maxed = st.sem("maxed")
    exped = st.sem("exped")
    combined = st.sem("combined")
    turned = st.sem("turned")
    turn_copied = st.sem("turn_copied")
    summed = st.sem("summed")
    o_copied = st.sem("o_copied")
    squared = st.sem("squared")
    meaned, rooted, scaled = st.sem("meaned"), st.sem("rooted"), st.sem("scaled")
    y_turned, y_copied = st.sem("y_turned"), st.sem("y_copied")
    chain_sem = st.sem("chain")
    PAIRS = DA_HEADS * TILES
    SCALE = DA_DIM ** -0.5

    with nc.Block() as block:
        @block.sync
        def _(sp):
            sp.dma_start(lam_in[:, :, :], dram["da_lambda"].partition_broadcast(P)).then_inc(small_in, 16)
            sp.dma_start(subln[:, 0:1], dram["da_subln_g"]).then_inc(small_in, 16)

        @block.tensor
        def _(pe):
            def scores(n, m):
                u = 2 * n + m
                h, t = n // TILES, n % TILES
                at_least(pe, exped, u - SCORES + 1)
                rows = slice(m * DA_DIM, (m + 1) * DA_DIM)
                for half in range(2):
                    last = nc.tensor.matmul(score[u % SCORES][:, half * WIDTH:(half + 1) * WIDTH],
                                            qkv["q_t"][rows, h, t * P:(t + 1) * P],
                                            qkv["k_t"][rows, h, half * WIDTH:(half + 1) * WIDTH], start=True, stop=True)
                last.then_inc(scored, 1)

            def turn(n, half):
                pe.wait_ge(combined, n + 1)
                at_least(pe, turn_copied, 2 * n + half)
                for i in range(4):
                    k = half * 4 + i
                    last = nc.tensor.transpose(turn_ps[:, i, :], prob[(2 * n) % PROBS][:, k * P:(k + 1) * P], ident[:, :])
                last.then_inc(turned, 1)

            scores(0, 0)
            scores(0, 1)
            scores(1, 0)
            for n in range(PAIRS):
                if n + 1 < PAIRS:
                    scores(n + 1, 1)
                turn(n, 0)
                if n + 2 < PAIRS:
                    scores(n + 2, 0)
                turn(n, 1)
                at_least(pe, o_copied, n)
                at_least(pe, squared, n)
                for k in range(TILES):
                    if k % 4 == 0:
                        pe.wait_ge(turn_copied, 2 * n + k // 4 + 1)
                    last = nc.tensor.matmul(o_ps[:, 0:P], diff_t[:, k, :], qkv["v"][:, k, (n // TILES) * P:(n // TILES + 1) * P],
                                            start=(k == 0), stop=(k == TILES - 1))
                last.then_inc(summed, 1)
            for t in range(TILES):
                pe.wait_ge(scaled, t + 1)
                at_least(pe, y_copied, t)
                for h in range(DA_HEADS):
                    last = nc.tensor.transpose(turn_ps[:, h, :], o[:, t, h, :], ident[:, :])
                last.then_inc(y_turned, 1)

        @block.scalar
        def _(act):
            def exponentials(n, m):
                u = 2 * n + m
                r = u % PROBS
                act.wait_ge(maxed, u + 1)
                if n >= 2:
                    act.wait_ge(turned, 2 * (n - 1))
                nc.scalar.activation(prob[r][:, :], score[u % SCORES][:, :], ACT.Exp, bias=neg[:, r:r + 1], scale=SCALE,
                                     accum_out=z[:, r:r + 1]).then_inc(exped, 1)

            def copy_turned(n, half):
                act.wait_ge(turned, 2 * n + half + 1)
                if half == 0:
                    at_least(act, summed, n)
                nc.scalar.activation(diff_t[:, 4 * half:4 * half + 4, :], turn_ps[:, :, :], ACT.Copy).then_inc(turn_copied, 1)

            act.wait_ge(lam_sum, 1)
            nc.scalar.activation(lam[:, 2:4], lam[:, 0:2], ACT.Exp).then_inc(lam_exp, 1)
            exponentials(0, 0)
            exponentials(0, 1)
            exponentials(1, 0)
            for n in range(PAIRS):
                copy_turned(n, 0)
                if n + 1 < PAIRS:
                    exponentials(n + 1, 1)
                copy_turned(n, 1)
                if n + 2 < PAIRS:
                    exponentials(n + 2, 0)
                h, t = n // TILES, n % TILES
                act.wait_ge(summed, n + 1)
                nc.scalar.activation(o[:, t, h, :], o_ps[:, 0:P], ACT.Copy).then_inc(o_copied, 1)
                nc.scalar.activation(square[:, :], o_ps[:, 0:P], ACT.Square,
                                     accum_out=sum_sq[:, t, h:h + 1]).then_inc(squared, 1)
            act.wait_ge(meaned, 1)
            nc.scalar.activation(rstd[:, 1, :, :], rstd[:, 0, :, :], ACT.Sqrt).then_inc(rooted, 1)
            for t in range(TILES):
                act.wait_ge(y_turned, t + 1)
                nc.scalar.activation(y_t[:, 0:DA_HEADS, t * P:(t + 1) * P], turn_ps[:, :, :], ACT.Copy,
                                     scale=subln[:, 1:2]).then_inc(y_copied, 1)

        @block.vector
        def _(dve):
            v = nc.vector
            chain = Chain(dve, chain_sem)

            def maximum(n, m):
                u = 2 * n + m
                r = u % PROBS
                dve.wait_ge(scored, u + 1)
                chain.step(v.reduce_max(top[:, r:r + 1], score[u % SCORES][:, :], AX.X))
                at_least(dve, exped, u - PROBS + 1)
                v.tensor_scalar(neg[:, r:r + 1], top[:, r:r + 1], -SCALE, None, ALU.mult).then_inc(maxed, 1)

            dve.wait_ge(small_in, 32)
            for i in range(2):
                last = v.tensor_tensor(lam_prod[:, i, :], lam_in[:, 2 * i, :], lam_in[:, 2 * i + 1, :], ALU.mult)
            chain.step(last)
            v.tensor_reduce(lam[:, 0:2], lam_prod[:, :, :], AX.X, ALU.add).then_inc(lam_sum, 1)
            dve.wait_ge(lam_exp, 1)
            chain.step(v.tensor_tensor(lam[:, 0:1], lam[:, 2:3], lam[:, 3:4], ALU.subtract))
            chain.step(v.tensor_scalar(lam[:, 1:2], lam[:, 0:1], -1.0, -LAMBDA_INIT, ALU.mult, ALU.add))
            v.tensor_scalar(subln[:, 1:2], subln[:, 0:1], 1.0 - LAMBDA_INIT, None, ALU.mult)
            maximum(0, 0)
            maximum(0, 1)
            maximum(1, 0)
            for n in range(PAIRS):
                a, b = (2 * n) % PROBS, (2 * n + 1) % PROBS
                dve.wait_ge(exped, 2 * n + 2)
                chain.step(v.reciprocal(rz[:, a:a + 2], z[:, a:a + 2]))
                v.tensor_scalar(prob[a][:, :], prob[a][:, :], rz[:, a:a + 1], None, ALU.mult)
                chain.step(v.tensor_scalar(rz[:, b:b + 1], rz[:, b:b + 1], lam[:, 1:2], None, ALU.mult))
                v.scalar_tensor_tensor(prob[a][:, :], prob[b][:, :], rz[:, b:b + 1], prob[a][:, :],
                                       ALU.mult, ALU.add).then_inc(combined, 1)
                if n + 1 < PAIRS:
                    maximum(n + 1, 1)
                if n + 2 < PAIRS:
                    maximum(n + 2, 0)
            dve.wait_ge(o_copied, PAIRS)
            dve.wait_ge(squared, PAIRS)
            v.tensor_scalar(rstd[:, 0, :, :], sum_sq[:, :, :], 1.0 / P, LN_EPS, ALU.mult, ALU.add).then_inc(meaned, 1)
            dve.wait_ge(rooted, 1)
            chain.step(v.reciprocal(rstd[:, 0, :, :], rstd[:, 1, :, :]))
            for t in range(TILES):
                v.tensor_tensor(o[:, t, :, :], o[:, t, :, :], rstd[:, 0, t, :].unsqueeze(2).to_broadcast([P, DA_HEADS, P]),
                                ALU.mult).then_inc(scaled, 1)


def shared(nc, ctx):
    st = Stage(nc, ctx, "all")
    consts = {"ident": st.sb("ident", [P, P]), "iota": st.sb("iota", [P, N_KEYS])}
    mix_t = st.sb("mix_t", [P, KT, SEQ])
    return consts, mix_t


def shared_tables(nc, ctx):
    st = Stage(nc, ctx, "tables")
    return {"cos": st.sb("cos", [P, TILES, ROPE_HALF]), "sin": st.sb("sin", [P, TILES, ROPE_HALF]),
            "mask": st.sb("mask", [P, 2, P]), "pick": st.sb("pick", [ML_HEADS, ML_HEADS, P])}


def shared_ml(nc, ctx):
    st = Stage(nc, ctx, "ml")
    return {"q_t": st.sb("q_t", [P, ML_HEADS, SEQ]), "k_t": st.sb("k_t", [P, ML_HEADS, SEQ]),
            "v": st.sb("v", [P, TILES, ML_HEADS, ML_DIM + 1]), "o": st.sb("o", [P, TILES, WIDTH]),
            "gates": st.sb("gates", [P, TILES, 16])}


def shared_qkv(nc, ctx):
    st = Stage(nc, ctx, "da")
    return {"q_t": st.sb("q_t", [P, DA_HEADS, SEQ]), "k_t": st.sb("k_t", [P, DA_HEADS, SEQ]),
            "v": st.sb("v", [P, TILES, WIDTH])}


def mlstm_stage(nc, st, consts, ml, y_t, dram):
    ident, mask, pick = consts["ident"], consts["mask"], consts["pick"]
    W_RING = 3
    run_max = [st.sb(f"run_max{d}", [ML_HEADS, SEQ]) for d in range(2)]
    u_cols = st.sb("u_cols", [P, 2, TILES, ML_HEADS])
    floor = st.sb("floor", [P, 2, TILES, ML_HEADS])
    norm_g = st.sb("norm_g", [P, ML_HEADS])

    with ExitStack() as rows_ctx:
        rows = Stage(nc, rows_ctx, "m_rows")
        i_row = [rows.sb(f"i{d}", [ML_HEADS, SEQ]) for d in range(2)]
        f_row = [rows.sb(f"f{d}", [ML_HEADS, SEQ]) for d in range(2)]
        b_row = [rows.sb(f"b{d}", [ML_HEADS, SEQ]) for d in range(2)]
        zeros = rows.sb("zeros", [ML_HEADS, SEQ])
        row_ps = [rows.ps(f"row{r}", [ML_HEADS, SEQ]) for r in range(3)]
        cols_ps = rows.ps("cols", [P, 2, 2, TILES, ML_HEADS])
        g_in, zeroed = rows.sem("g_in"), rows.sem("zeroed")
        turned, copied, ready, back, u_copied, chain_sem = (rows.sem(n) for n in ("turned", "copied", "ready", "back", "u_copied", "chain"))
        with nc.Block() as block:
            @block.sync
            def _(sp):
                sp.dma_start(norm_g[:, :], dram["ml_norm_g"]).then_inc(g_in, 16)
                sp.wait_ge(g_in, 16)

            @block.gpsimd
            def _(pool):
                nc.gpsimd.memset(zeros[:, :], 0.0).then_inc(zeroed, 1)

            @block.tensor
            def _(pe):
                for g in range(4):
                    if g == 3:
                        pe.wait_ge(copied, 1)
                    for t in range(TILES):
                        last = nc.tensor.transpose(row_ps[g % 3][:, t * P:(t + 1) * P],
                                                   ml["gates"][:, t, g * ML_HEADS:(g + 1) * ML_HEADS], ident[:, :])
                    last.then_inc(turned, 1)
                for d in range(2):
                    pe.wait_ge(ready, d + 1)
                    for t in range(TILES):
                        nc.tensor.transpose(cols_ps[:, 0, d, t, :], i_row[d][:, t * P:(t + 1) * P], ident[0:ML_HEADS, 0:ML_HEADS])
                        last = nc.tensor.transpose(cols_ps[:, 1, d, t, :], b_row[d][:, t * P:(t + 1) * P],
                                                   ident[0:ML_HEADS, 0:ML_HEADS])
                    last.then_inc(back, 1)

            @block.scalar
            def _(act):
                act.wait_ge(back, 2)
                act.wait_ge(u_copied, 1)
                nc.scalar.activation(floor[:, :, :, :], cols_ps[:, 1, :, :, :], ACT.Exp, scale=-1.0)

            @block.vector
            def _(dve):
                v = nc.vector
                chain = Chain(dve, chain_sem)
                for g in range(4):
                    dve.wait_ge(turned, g + 1)
                    dst = (i_row if g % 2 == 0 else f_row)[g // 2]
                    v.tensor_copy(dst[:, :], row_ps[g % 3][:, :]).then_inc(copied, 1)
                dve.wait_ge(copied, 4)
                dve.wait_ge(zeroed, 1)

                def along(row, d):
                    return row[:, :] if d == 0 else row[:, ::-1]

                for d in range(2):
                    chain.step(v.tensor_tensor_scan(along(b_row[d], d), along(f_row[d], d), zeros[:, :], 0.0, ALU.add, ALU.add))
                    chain.step(v.tensor_tensor(i_row[d][:, :], i_row[d][:, :], b_row[d][:, :], ALU.subtract))
                    chain.step(v.tensor_tensor_scan(along(run_max[d], d), along(i_row[d], d), along(i_row[d], d), NEG, ALU.max, ALU.max))
                    v.tensor_tensor(b_row[d][:, :], b_row[d][:, :], run_max[d][:, :], ALU.add).then_inc(ready, 1)
                dve.wait_ge(back, 2)
                v.tensor_copy(u_cols[:, :, :, :], cols_ps[:, 0, :, :, :]).then_inc(u_copied, 1)

    both = st.sb("both", [P, TILES, SEQ])
    diag_b = st.sb("diag_b", [P, TILES, P])
    max_b = [st.sb(f"max_b{d}", [P, SEQ]) for d in range(2)]
    max_diag = [st.sb(f"max_diag{d}", [P, TILES, P]) for d in range(2)]
    weight = [st.sb(f"weight{r}", [P, SEQ + P]) for r in range(W_RING)]
    h_sum = st.sb("h_sum", [P, TILES, ML_HEADS, ML_DIM])
    dens = [st.sb(f"den{r}", [P, 2]) for r in range(2)]
    stats = st.sb("stats", [P, TILES, ML_HEADS, 6])
    mean_var = st.sb("mean_var", [P, TILES, ML_HEADS, 2])
    rstd = st.sb("rstd", [P, 2, TILES, ML_HEADS])
    score = [st.ps(f"score{r}", [P, SEQ]) for r in range(2)]
    spread_ps = [st.ps(f"spread{r}", [P, WIDTH]) for r in range(2)]
    h_ps = [st.ps(f"h{r}", [P, 2, ML_DIM + 1]) for r in range(2)]
    names = "spread spread_copied masked weighed scored applied summed h_read std rooted gated turned y_copied chain normed".split()
    s = {n: st.sem(n) for n in names}
    K_SCALE = ML_DIM ** -0.5
    HT = ML_HEADS * TILES

    with nc.Block() as block:
        @block.tensor
        def _(pe):
            def spread(h):
                for i in range(4):
                    d, half = i // 2, i % 2
                    n = 4 * h + i
                    at_least(pe, s["spread_copied"], n - 1)
                    nc.tensor.matmul(spread_ps[n % 2][:, :], pick[:, h, :], run_max[d][:, half * WIDTH:(half + 1) * WIDTH],
                                     start=True, stop=True).then_inc(s["spread"], 1)

            def scores(h, i):
                n = h * TILES + i
                at_least(pe, s["applied"], n - 1)
                for half in range(2):
                    last = nc.tensor.matmul(score[n % 2][:, half * WIDTH:(half + 1) * WIDTH], ml["k_t"][:, h, i * P:(i + 1) * P],
                                            ml["q_t"][:, h, half * WIDTH:(half + 1) * WIDTH], start=True, stop=True)
                last.then_inc(s["scored"], 1)

            def sums(h, j):
                n = h * TILES + j
                at_least(pe, s["h_read"], n - 1)
                for l in range(j + 1):
                    nc.tensor.matmul(h_ps[n % 2][:, 0, :], both[:, l, j * P:(j + 1) * P], ml["v"][:, l, h, :],
                                     start=(l == 0), stop=(l == j))
                for l in range(j, TILES):
                    lhs = diag_b[:, l, :] if l == j else both[:, l, j * P:(j + 1) * P]
                    last = nc.tensor.matmul(h_ps[n % 2][:, 1, :], lhs, ml["v"][:, l, h, :], start=(l == j), stop=(l == TILES - 1))
                last.then_inc(s["summed"], 1)

            spread(0)
            for h in range(ML_HEADS):
                for i in range(TILES):
                    scores(h, i)
                if h + 1 < ML_HEADS:
                    spread(h + 1)
                pe.wait_ge(s["applied"], (h + 1) * TILES)
                for j in range(TILES):
                    sums(h, j)
            for t in range(TILES):
                pe.wait_ge(s["gated"], t + 1)
                at_least(pe, s["y_copied"], t - 1)
                for h in range(ML_HEADS):
                    last = nc.tensor.transpose(score[t % 2][:, h * P:(h + 1) * P], h_sum[:, t, h, :], ident[:, :])
                last.then_inc(s["turned"], 1)

        @block.scalar
        def _(act):
            for h in range(ML_HEADS):
                if h >= 1:
                    act.wait_ge(s["weighed"], TILES * h)
                    act.wait_ge(s["masked"], 2 * h)
                for i in range(4):
                    n = 4 * h + i
                    act.wait_ge(s["spread"], n + 1)
                    nc.scalar.activation(max_b[i // 2][:, (i % 2) * WIDTH:(i % 2 + 1) * WIDTH], spread_ps[n % 2][:, :],
                                         ACT.Copy).then_inc(s["spread_copied"], 1)
                act.wait_ge(s["spread_copied"], 4 * h + 4)
                act.wait_ge(s["masked"], 2 * h + 2)
                for i in range(TILES):
                    n = h * TILES + i
                    at_least(act, s["applied"], n - W_RING + 1)
                    w = weight[n % W_RING]
                    u = [u_cols[:, d, i, h:h + 1] for d in range(2)]
                    if i > 0:
                        nc.scalar.activation(w[:, 0:i * P], max_b[1][:, 0:i * P], ACT.Exp, bias=u[1], scale=-1.0)
                    if i + 1 < TILES:
                        nc.scalar.activation(w[:, (i + 1) * P:SEQ], max_b[0][:, (i + 1) * P:SEQ], ACT.Exp, bias=u[0], scale=-1.0)
                    nc.scalar.activation(w[:, i * P:(i + 1) * P], max_diag[0][:, i, :], ACT.Exp, bias=u[0], scale=-1.0)
                    nc.scalar.activation(w[:, SEQ:SEQ + P], max_diag[1][:, i, :], ACT.Exp, bias=u[1],
                                         scale=-1.0).then_inc(s["weighed"], 1)
            act.wait_ge(s["std"], 1)
            nc.scalar.activation(rstd[:, 1, :, :], rstd[:, 0, :, :], ACT.Sqrt).then_inc(s["rooted"], 1)
            for t in range(TILES):
                act.wait_ge(s["turned"], t + 1)
                for h in range(ML_HEADS):
                    last = nc.scalar.activation(y_t[:, ML_HEADS + h, t * P:(t + 1) * P], score[t % 2][:, h * P:(h + 1) * P],
                                                ACT.Copy, scale=norm_g[:, h:h + 1])
                last.then_inc(s["y_copied"], 1)

        @block.vector
        def _(dve):
            v = nc.vector
            chain = Chain(dve, s["chain"])
            for h in range(ML_HEADS):
                for d in range(2):
                    dve.wait_ge(s["spread_copied"], 4 * h + 2 * d + 2)
                    if h >= 1:
                        dve.wait_ge(s["weighed"], TILES * h)
                    v.tensor_tensor(max_diag[d][:, :, :], max_b[d][:, :].rearrange("p (t j) -> p t j", j=P),
                                    mask[:, d, :].unsqueeze(1).to_broadcast([P, TILES, P]), ALU.add).then_inc(s["masked"], 1)
                for i in range(TILES):
                    n = h * TILES + i
                    dve.wait_ge(s["scored"], n + 1)
                    dve.wait_ge(s["weighed"], n + 1)
                    at_least(dve, s["summed"], h * TILES)
                    v.scalar_tensor_tensor(diag_b[:, i, :], score[n % 2][:, i * P:(i + 1) * P], K_SCALE,
                                           weight[n % W_RING][:, SEQ:SEQ + P], ALU.mult, ALU.mult)
                    v.scalar_tensor_tensor(both[:, i, :], score[n % 2][:, :], K_SCALE, weight[n % W_RING][:, 0:SEQ],
                                           ALU.mult, ALU.mult).then_inc(s["applied"], 1)
                for j in range(TILES):
                    n = h * TILES + j
                    dve.wait_ge(s["summed"], n + 1)
                    at_least(dve, s["h_read"], n - 1)
                    bank, den = h_ps[n % 2], dens[n % 2]
                    chain.step(v.tensor_tensor(den[:, :], bank[:, :, ML_DIM], floor[:, :, j, h], ALU.max))
                    chain.step(v.scalar_tensor_tensor(den[:, :], bank[:, :, ML_DIM], -1.0, den[:, :], ALU.mult, ALU.max))
                    chain.step(v.reciprocal(den[:, :], den[:, :]))
                    chain.step(v.tensor_scalar(h_sum[:, j, h, :], bank[:, 0, 0:ML_DIM], den[:, 0:1], None, ALU.mult))
                    v.scalar_tensor_tensor(h_sum[:, j, h, :], bank[:, 1, 0:ML_DIM], den[:, 1:2], h_sum[:, j, h, :],
                                           ALU.mult, ALU.add).then_inc(s["h_read"], 1)
                dve.wait_ge(s["h_read"], (h + 1) * TILES)
            for j in range(TILES):
                for h in range(ML_HEADS):
                    last = v.bn_stats(stats[:, j, h, :], h_sum[:, j, h, :])
            chain.step(last)
            for j in range(TILES):
                for h in range(ML_HEADS):
                    last = v.bn_aggr(mean_var[:, j, h, :], stats[:, j, h, :])
            chain.step(last)
            v.tensor_scalar(rstd[:, 0, :, :], mean_var[:, :, :, 1], LN_EPS, None, ALU.add).then_inc(s["std"], 1)
            dve.wait_ge(s["rooted"], 1)
            chain.step(v.reciprocal(rstd[:, 0, :, :], rstd[:, 1, :, :]))
            for j in range(TILES):
                for h in range(ML_HEADS):
                    last = v.tensor_scalar(h_sum[:, j, h, :], h_sum[:, j, h, :], mean_var[:, j, h, 0:1], rstd[:, 0, j, h:h + 1],
                                           ALU.subtract, ALU.mult)
                chain.step(last)
                v.tensor_tensor(h_sum[:, j, :, :], h_sum[:, j, :, :], ml["o"][:, j, :].rearrange("p (h e) -> p h e", h=ML_HEADS),
                                ALU.mult).then_inc(s["gated"], 1)


def merge_stage(nc, st, consts, mix_t, dram, x1_rows):
    ident = consts["ident"]
    x_low, x_high = st.sb("x_low", [P, KT, SEQ], F32R), st.sb("x_high", [P, KT, SEQ], F32R)
    w_branch = [st.sb(f"w_branch{r}", [P, 4, 2, P]) for r in range(2)]
    merged = st.sb("merged", [P, KT, SEQ])
    w_raw = [st.sb(f"w_raw{r}", [P, KT, 2, P]) for r in range(2)]
    w_low = [st.sb(f"w_low{r}", [P, KT, 2, P], F32R) for r in range(2)]
    w_high = [st.sb(f"w_high{r}", [P, KT, 2, P], F32R) for r in range(2)]
    sig = st.sb("sig", [P, 2, WIDTH])
    prod = st.sb("prod", [P, 2, WIDTH])
    bank = [st.ps(f"bank{r}", [P, WIDTH]) for r in range(8)]
    x_in, ln_in = st.sem("x_in"), st.sem("ln_in")
    g_in = [st.sem(f"g_in{r}") for r in range(2)]
    gate_full, branch_full, sig_done, mixed, merged_done, chain_sem = (
        st.sem(n) for n in ("gate_full", "branch_full", "sig_done", "mixed", "merged_done", "chain"))
    x_highs, x_split = st.sem("x_highs"), st.sem("x_split")
    w_highs, w_split = st.sem("w_highs"), st.sem("w_split")
    UNITS = 2 * KT

    def high_part(high, value):
        return nc.scalar.activation(high, value, ACT.Copy)

    def low_part(low, value, high):
        return nc.vector.tensor_tensor(low, value, high.bitcast(F32), ALU.subtract)

    def three_passes(out, lhs_high, lhs_low, rhs_high, rhs_low, start, stop):
        nc.tensor.matmul(out, lhs_high, rhs_high, start=start, stop=False)
        nc.tensor.matmul(out, lhs_high, rhs_low, start=False, stop=False)
        return nc.tensor.matmul(out, lhs_low, rhs_high, start=False, stop=stop)

    w_out_low, w_out_high = x_low, x_high
    out_in = [st.sem(f"out_in{r}") for r in range(2)]

    def raw_w_out(k):
        return w_raw[k // 2 % 2][:, 4 * (k % 2):4 * (k % 2 + 1), :, :].rearrange("p a b c -> p (a b c)")

    def load_w_out(sp, j):
        for k in (2 * j, 2 * j + 1):
            sp.dma_start(raw_w_out(k), dram["w_out"][k * P:(k + 1) * P, :]).then_inc(out_in[j % 2], 16)

    with nc.Block() as block:
        @block.sync
        def _(sp):
            w_view = dram["w_in"].rearrange("(k p) n -> p k n", p=P)

            def columns(c):
                at_least(sp, w_split, c - 1)
                at_least(sp, branch_full, 2 * (c - 1))
                for b, name in enumerate(("w_a", "w_m")):
                    col = COL_BRANCH + b * D_MODEL + c * P
                    sp.dma_start(w_raw[c % 2][:, :, b, :], w_view[:, :, col:col + P]).then_inc(g_in[c % 2], 16)
                    sp.dma_start(w_branch[c % 2][:, :, b, :], dram[name].rearrange("(k p) n -> p k n", p=P)[:, :, c * P:(c + 1) * P]
                                 ).then_inc(g_in[c % 2], 16)

            columns(0)
            for k in range(KT):
                sp.dma_start(merged[:, k, :], dram["x_t"][k * P:(k + 1) * P, :]).then_inc(x_in, 16)
            for c in range(1, KT):
                columns(c)
            sp.wait_ge(w_split, KT)
            for j in range(2):
                load_w_out(sp, j)

        @block.tensor
        def _(pe):
            for n in range(UNITS):
                c, half = n // 2, n % 2
                cols = slice(half * WIDTH, (half + 1) * WIDTH)
                at_least(pe, mixed, n - 1)
                pe.wait_ge(w_split, c + 1)
                for b in range(2):
                    for k in range(KT):
                        if n == 0 and b == 0:
                            pe.wait_ge(x_split, k + 1)
                        last = three_passes(bank[4 * (n % 2) + b][:, :], w_high[c % 2][:, k, b, :], w_low[c % 2][:, k, b, :],
                                            x_high[:, k, cols], x_low[:, k, cols], k == 0, k == KT - 1)
                last.then_inc(gate_full, 1)
                for b in range(2):
                    for k in range(4):
                        last = nc.tensor.matmul(bank[4 * (n % 2) + 2 + b][:, :], w_branch[c % 2][:, k, b, :],
                                                mix_t[:, 4 * b + k, cols], start=(k == 0), stop=(k == 3))
                last.then_inc(branch_full, 1)

        @block.scalar
        def _(act):
            def gate_columns_high(c):
                act.wait_ge(g_in[c % 2], 64 * (c // 2 + 1))
                at_least(act, gate_full, 2 * (c - 1))
                high_part(w_high[c % 2][:, :, :, :], w_raw[c % 2][:, :, :, :]).then_inc(w_highs, 1)

            gate_columns_high(0)
            act.wait_ge(x_in, 16 * KT)
            for k in range(KT):
                high_part(x_high[:, k, :], merged[:, k, :]).then_inc(x_highs, 1)
            for n in range(UNITS):
                if n % 2 == 0 and n // 2 + 1 < KT:
                    gate_columns_high(n // 2 + 1)
                act.wait_ge(gate_full, n + 1)
                at_least(act, mixed, n)
                for b in range(2):
                    last = nc.scalar.activation(sig[:, b, :], bank[4 * (n % 2) + b][:, :], ACT.Sigmoid)
                last.then_inc(sig_done, 1)

        @block.vector
        def _(dve):
            v = nc.vector

            def gate_columns_low(c):
                dve.wait_ge(w_highs, c + 1)
                low_part(w_low[c % 2][:, :, :, :], w_raw[c % 2][:, :, :, :], w_high[c % 2][:, :, :, :]).then_inc(w_split, 1)

            gate_columns_low(0)
            for k in range(KT):
                dve.wait_ge(x_highs, k + 1)
                low_part(x_low[:, k, :], merged[:, k, :], x_high[:, k, :]).then_inc(x_split, 1)
            for n in range(UNITS):
                c, half = n // 2, n % 2
                if half == 0 and c + 1 < KT:
                    gate_columns_low(c + 1)
                dve.wait_ge(branch_full, n + 1)
                dve.wait_ge(sig_done, n + 1)
                at_least(dve, merged_done, n)
                if n == 0:
                    dve.wait_ge(x_split, KT)
                for b in range(2):
                    last = v.tensor_tensor(prod[:, b, :], sig[:, b, :], bank[4 * (n % 2) + 2 + b][:, :], ALU.mult)
                last.then_inc(mixed, 1)
                dve.wait_ge(mixed, n + 1)
                v.tensor_tensor(merged[:, c, half * WIDTH:(half + 1) * WIDTH], prod[:, 0, :], prod[:, 1, :],
                                ALU.add).then_inc(merged_done, 1)

    m_high = [b[:, :, 0, :] for b in w_high]
    m_low = [b[:, :, 0, :] for b in w_low]
    out_highs, out_split = st.sem("out_highs"), st.sem("out_split")
    m_highs, m_split = st.sem("m_highs"), st.sem("m_split")
    ln_gain, ln_offset = st.sb("ln_gain", [P, D_MODEL]), st.sb("ln_offset", [P, D_MODEL])
    ln_g, ln_b = ln_gain[:, :], ln_offset[:, :]
    x_row = [b[:, :, :].rearrange("p a b -> p (a b)") for b in (sig, prod)]
    r_row = [b[:, :, :, :].rearrange("p a b c -> p (a b c)") for b in w_branch]
    stats = st.sb("stats", [P, 2, 6])
    mean_var = st.sb("mean_var", [P, 2])
    rstd = st.sb("rstd", [P, 2])
    full, read, var_done, rooted, normed, turned, turn_copied = (
        st.sem(n) for n in ("full", "read", "var_done", "rooted", "normed", "turned", "turn_copied"))
    xr = [st.sem(f"xr{r}") for r in range(2)]
    stored = [st.sem(f"stored{r}") for r in range(2)]
    with nc.Block() as block:
        @block.sync
        def _(sp):
            sp.dma_start(x_row[0], dram["x"][0:P, :]).then_inc(xr[0], 16)
            sp.dma_start(x_row[1], dram["x"][P:2 * P, :]).then_inc(xr[1], 16)
            sp.dma_start(ln_g, dram["ln1_g"].partition_broadcast(P)).then_inc(ln_in, 16)
            sp.dma_start(ln_b, dram["ln1_b"].partition_broadcast(P)).then_inc(ln_in, 16)
            for j in range(2, KT // 2):
                sp.wait_ge(out_split, 2 * (j - 1))
                load_w_out(sp, j)
            for t in range(TILES):
                sp.wait_ge(normed, t + 1)
                sp.dma_start(x1_rows[t * P:(t + 1) * P, :], r_row[t % 2]).then_inc(stored[t % 2], 16)
                if t + 2 < TILES:
                    sp.dma_start(x_row[t % 2], dram["x"][(t + 2) * P:(t + 3) * P, :]).then_inc(xr[t % 2], 16)
            for r in range(2):
                sp.wait_ge(stored[r], 16 * TILES // 2)

        @block.tensor
        def _(pe):
            def turn(t):
                pe.wait_ge(normed, t + 1)
                for half in range(2):
                    n = 2 * t + half
                    at_least(pe, turn_copied, n - 1)
                    for i in range(4):
                        k = half * 4 + i
                        last = nc.tensor.transpose(bank[4 + half][:, i * P:(i + 1) * P], r_row[t % 2][:, k * P:(k + 1) * P], ident[:, :])
                    last.then_inc(turned, 1)

            for t in range(TILES):
                at_least(pe, read, t - 1)
                pe.wait_ge(m_split, t + 1)
                for half in range(2):
                    cols = slice(half * WIDTH, (half + 1) * WIDTH)
                    for k in range(KT):
                        if t == 0 and half == 0:
                            pe.wait_ge(out_split, k + 1)
                        last = three_passes(bank[2 * (t % 2) + half][:, :], m_high[t % 2][:, k, :], m_low[t % 2][:, k, :],
                                            w_out_high[:, k, cols], w_out_low[:, k, cols], k == 0, k == KT - 1)
                last.then_inc(full, 1)
                if t >= 1:
                    turn(t - 1)
            turn(TILES - 1)

        @block.scalar
        def _(act):
            def tokens_high(t):
                at_least(act, full, t - 1)
                nc.scalar.activation(m_high[t % 2], merged[:, :, t * P:(t + 1) * P], ACT.Copy).then_inc(m_highs, 1)

            tokens_high(0)
            for k in range(KT):
                act.wait_ge(out_in[k // 2 % 2], 32 * (k // 4 + 1))
                high_part(w_out_high[:, k, :], raw_w_out(k)).then_inc(out_highs, 1)
            for t in range(TILES):
                if t + 1 < TILES:
                    tokens_high(t + 1)
                act.wait_ge(var_done, t + 1)
                nc.scalar.activation(rstd[:, 1:2], rstd[:, 0:1], ACT.Sqrt).then_inc(rooted, 1)
                for half in range(2):
                    act.wait_ge(turned, 2 * t + half + 1)
                    nc.scalar.activation(mix_t[:, 4 * half:4 * half + 4, t * P:(t + 1) * P],
                                         bank[4 + half][:, :].rearrange("p (k c) -> p k c", k=4), ACT.Copy).then_inc(turn_copied, 1)

        @block.vector
        def _(dve):
            v = nc.vector
            chain = Chain(dve, chain_sem)
            def tokens_low(t):
                dve.wait_ge(m_highs, t + 1)
                v.tensor_tensor(m_low[t % 2], merged[:, :, t * P:(t + 1) * P], m_high[t % 2].bitcast(F32),
                                ALU.subtract).then_inc(m_split, 1)

            tokens_low(0)
            for k in range(KT):
                dve.wait_ge(out_highs, k + 1)
                low_part(w_out_low[:, k, :], raw_w_out(k), w_out_high[:, k, :]).then_inc(out_split, 1)
            dve.wait_ge(ln_in, 32)
            for t in range(TILES):
                if t + 1 < TILES:
                    tokens_low(t + 1)
                dve.wait_ge(full, t + 1)
                dve.wait_ge(xr[t % 2], 16 * (t // 2 + 1))
                at_least(dve, stored[t % 2], 16 * (t // 2))
                at_least(dve, turned, 2 * (t - 1))
                r = r_row[t % 2]
                for half in range(2):
                    cols = slice(half * WIDTH, (half + 1) * WIDTH)
                    last = v.scalar_tensor_tensor(r[:, cols], x_row[t % 2][:, cols], DN_ALPHA, bank[2 * (t % 2) + half][:, :],
                                                  ALU.mult, ALU.add)
                last.then_inc(read, 1)
                dve.wait_ge(read, t + 1)
                for half in range(2):
                    last = v.bn_stats(stats[:, half, :], r[:, half * WIDTH:(half + 1) * WIDTH])
                chain.step(last)
                chain.step(v.bn_aggr(mean_var[:, :], stats[:, :, :].rearrange("p a b -> p (a b)")))
                v.tensor_scalar(rstd[:, 0:1], mean_var[:, 1:2], LN_EPS, None, ALU.add).then_inc(var_done, 1)
                dve.wait_ge(rooted, t + 1)
                chain.step(v.reciprocal(rstd[:, 0:1], rstd[:, 1:2]))
                chain.step(v.tensor_scalar(r, r, mean_var[:, 0:1], rstd[:, 0:1], ALU.subtract, ALU.mult))
                chain.step(v.tensor_tensor(r, r, ln_g, ALU.mult))
                v.tensor_tensor(r, r, ln_b, ALU.add).then_inc(normed, 1)


def layer_program(nc, dram, x1_rows, gates_dram, out_rows):
    with ExitStack() as ctx:
        consts, mix_t = shared(nc, ctx)
        with ExitStack() as ml_ctx:
            consts.update(shared_tables(nc, ml_ctx))
            ml = shared_ml(nc, ml_ctx)
            with ExitStack() as qkv_ctx:
                qkv = shared_qkv(nc, qkv_ctx)
                with ExitStack() as stage_ctx:
                    project_stage(nc, Stage(nc, stage_ctx, "proj"), consts, mix_t, ml, qkv, dram)
                with ExitStack() as stage_ctx:
                    attention_stage(nc, Stage(nc, stage_ctx, "attn"), consts, qkv, mix_t, dram)
            with ExitStack() as stage_ctx:
                mlstm_stage(nc, Stage(nc, stage_ctx, "mlstm"), consts, ml, mix_t, dram)
        with ExitStack() as stage_ctx:
            merge_stage(nc, Stage(nc, stage_ctx, "merge"), consts, mix_t, dram, x1_rows)
        routes = shared_routes(nc, ctx)
        with ExitStack() as stage_ctx:
            route_stage(nc, Stage(nc, stage_ctx, "route"), consts, mix_t, routes, dram, x1_rows, out_rows)
        with ExitStack() as stage_ctx:
            experts_stage(nc, Stage(nc, stage_ctx, "experts"), consts, mix_t, routes, dram, x1_rows, gates_dram, out_rows)


def shape_constants():
    position = np.arange(SEQ, dtype=np.float32)
    inv_freq = np.float32(ROPE_THETA) ** (-np.arange(0, 2 * ROPE_HALF, 2, dtype=np.float32) / np.float32(2 * ROPE_HALF))
    angle = (position[:, None] * inv_freq[None, :]).reshape(TILES, P, ROPE_HALF).transpose(1, 0, 2)
    step, row = np.arange(P)[:, None], np.arange(P)[None, :]
    mask = np.stack([np.where(row < step, BIG, 0.0), np.where(row > step, BIG, 0.0)], axis=1).astype(np.float32)
    pick = np.zeros((ML_HEADS, ML_HEADS, P), np.float32)
    for h in range(ML_HEADS):
        pick[h, h] = 1.0
    return {
        "ident": np.eye(P, dtype=np.float32),
        "iota": np.ascontiguousarray(np.broadcast_to(np.arange(N_KEYS, dtype=np.float32), (P, N_KEYS))),
        "cos": np.ascontiguousarray(np.cos(angle)),
        "sin": np.ascontiguousarray(np.sin(angle)),
        "mask": mask,
        "pick": pick,
    }


def kernel(**inputs):
    import concourse.bacc as _bacc
    from concourse.bass_utils import run_bass_kernel_spmd as _run

    a = {name: np.asarray(value) for name, value in inputs.items()}
    x = a["x"][0]
    laid = {
        "x": x,
        "x_t": x.T,
        "w_in": a["w_in"][0],
        "gate_b": a["ml_gate_b"].reshape(4 * ML_HEADS),
        "conv_w": a["ml_conv_w"][0].T.reshape(2 * ML_HEADS, P, CONV).transpose(1, 0, 2),
        "conv_b": a["ml_conv_b"][0].reshape(2 * ML_HEADS, P).T,
        "da_lambda": a["da_lambda"][0],
        "da_subln_g": a["da_subln_g"][0].reshape(P, 1),
        "ml_norm_g": a["ml_norm_g"][0].reshape(ML_HEADS, P).T,
        "w_a": a["w_branch_attn"][0],
        "w_m": a["w_branch_mlstm"][0],
        "w_out": a["w_out"][0],
        "ln1_g": a["ln1_g"][0],
        "ln1_b": a["ln1_b"][0],
        "w_q": a["peer_w_q"][0],
        "keys_t": a["peer_sub_keys"][0].transpose(0, 2, 1),
        "u": a["peer_u"][0],
        "u_t": a["peer_u"][0].reshape(N_KEYS, N_KEYS, KT, P).transpose(1, 3, 2, 0).reshape(N_KEYS * P, KT * N_KEYS),
        "v": a["peer_v"][0],
        "ln2_g": a["ln2_g"][0],
        "ln2_b": a["ln2_b"][0],
        **shape_constants(),
    }
    nc = _bacc.Bacc("TRN2", target_bir_lowering=False, num_devices=1)
    arrays, dram = {}, {}
    for name, value in laid.items():
        arrays[f"in_{name}"] = np.ascontiguousarray(value)
        dram[name] = nc.dram_tensor(f"in_{name}", value.shape, F32, kind="ExternalInput").ap()
    x1_rows = nc.dram_tensor("x1_rows", (SEQ, D_MODEL), F32, kind="Internal").ap()
    gates_dram = nc.dram_tensor("gates_by_expert", (N_DENSE // G_COLS * (N_KEYS // 2) * N_KEYS, 2 * G_COLS), F32, kind="Internal").ap()
    out_rows = nc.dram_tensor("out_rows", (SEQ, D_MODEL), F32, kind="ExternalOutput").ap()
    layer_program(nc, dram, x1_rows, gates_dram, out_rows)
    result = _run(nc, [arrays], core_ids=[0])
    return result.results[0]["out_rows"].reshape(1, SEQ, D_MODEL)
```
